# Optimizing a Trainium2 kernel written in Bass

```python
import jax, jax.numpy as jnp
from jax import lax
import numpy as np

D_MODEL = 1024
BATCH = 1
SEQ = 1024
DEPTH = 2

N_A = DEPTH // 2
N_B = DEPTH - N_A
N_HEADS = 16
HEAD_DIM = D_MODEL // N_HEADS
CONV_WIDTH = 3
D_FF = ((8 * D_MODEL // 3 + 255) // 256) * 256
DILATED_GROUPS = ((128, 1), (512, 4), (2048, 16))
BLOCK = 128
EPS = 1e-6

kernel_name = "yoco_shortconv_dilated_alibi_trunk"

def _rms_norm(x, g):
    xf = x.astype(jnp.float32)
    y = xf * lax.rsqrt(jnp.mean(xf * xf, axis=-1, keepdims=True) + EPS)
    return (y * g.astype(jnp.float32)).astype(x.dtype)

def _swiglu(x, w_in, w_out):
    gate, up = jnp.split(x @ w_in, 2, axis=-1)
    return (jax.nn.silu(gate) * up) @ w_out

def _short_conv(x, w_in, w_conv, w_out):
    b_gate, c_gate, h = jnp.split(x @ w_in, 3, axis=-1)
    u = c_gate * h
    u = lax.conv_general_dilated(
        u, w_conv[:, None, :].astype(u.dtype), window_strides=(1,),
        padding=[(CONV_WIDTH - 1, 0)],
        dimension_numbers=("NWC", "WIO", "NWC"),
        feature_group_count=D_MODEL)
    return (b_gate * u) @ w_out

def _alibi_slopes():
    h = np.arange(N_HEADS, dtype=np.float32) + 1.0
    return jnp.asarray(np.power(2.0, -8.0 * h / N_HEADS), dtype=jnp.float32)

def _strided_blocks(t, dilation):
    b, s, h, e = t.shape
    mult = dilation * BLOCK
    sp = -(-s // mult) * mult
    t = jnp.pad(t, ((0, 0), (0, sp - s), (0, 0), (0, 0)))
    return t.reshape(b, sp // mult, BLOCK, dilation, h, e)

def _with_prev_block(tb):
    prev = jnp.concatenate([jnp.zeros_like(tb[:, :1]), tb[:, :-1]], axis=1)
    return jnp.concatenate([prev, tb], axis=2)

def _shared_kv(h, g_kv, w_kv):
    b, s, _ = h.shape
    k, v = jnp.split(_rms_norm(h, g_kv) @ w_kv, 2, axis=-1)
    k = k.reshape(b, s, N_HEADS, HEAD_DIM)
    v = v.reshape(b, s, N_HEADS, HEAD_DIM)
    return [(_with_prev_block(_strided_blocks(k, d)), _with_prev_block(_strided_blocks(v, d)))
            for (_, d) in DILATED_GROUPS]

def _branch_attention(q, k_cat, v_cat, slopes, window, dilation):
    b, s, h, e = q.shape
    qb = _strided_blocks(q, dilation)
    nb = qb.shape[1]
    sc = jnp.einsum("bnqrhe,bnkrhe->bnrhqk", qb, k_cat).astype(jnp.float32)
    u = jnp.arange(BLOCK)[:, None]
    kk = jnp.arange(2 * BLOCK)[None, :]
    delta = u + BLOCK - kk
    band = (delta >= 0) & (delta <= window // dilation)
    first = (jnp.arange(nb) == 0)[:, None, None]
    valid = band[None] & ~(first & (kk < BLOCK)[None])
    bias = -slopes[:, None, None] * (delta * dilation).astype(jnp.float32)[None]
    sc = jnp.where(valid[:, None, None], sc + bias, -jnp.inf)
    m = jnp.max(sc, axis=-1, keepdims=True)
    p = jnp.exp(sc - m)
    den = jnp.sum(p, axis=-1, keepdims=True)
    o = jnp.einsum("bnrhqk,bnkrhe->bnqrhe", p / den, v_cat.astype(jnp.float32))
    lse = (m + jnp.log(den))[..., 0]
    o = o.reshape(b, nb * BLOCK * dilation, h, e)[:, :s]
    lse = lse.transpose(0, 1, 4, 2, 3).reshape(b, nb * BLOCK * dilation, h)[:, :s]
    return o, lse

def _dilated_attention(x, w_q, w_o, shared, slopes):
    b, s, _ = x.shape
    q = (x @ w_q).reshape(b, s, N_HEADS, HEAD_DIM) * (HEAD_DIM ** -0.5)
    outs, lses = [], []
    for (window, dil), (k_cat, v_cat) in zip(DILATED_GROUPS, shared):
        o, l = _branch_attention(q, k_cat, v_cat, slopes, window, dil)
        outs.append(o)
        lses.append(l)
    wts = jax.nn.softmax(jnp.stack(lses), axis=0)
    o = jnp.sum(wts[..., None] * jnp.stack(outs), axis=0)
    return o.reshape(b, s, D_MODEL).astype(x.dtype) @ w_o

def setup_inputs(seed: int = 0) -> dict:
    key = jax.random.key(seed)
    ks = jax.random.split(key, 12)
    f32 = jnp.float32
    nrm = lambda k, shape, fan_in: jax.random.normal(k, shape, f32) * (fan_in ** -0.5)
    return {
        "x": jax.random.normal(ks[0], (BATCH, SEQ, D_MODEL), f32),
        "norm_g": 1.0 + 0.05 * jax.random.normal(ks[1], (DEPTH, 4, D_MODEL), f32),
        "conv_in_w": nrm(ks[2], (N_A, D_MODEL, 3 * D_MODEL), D_MODEL),
        "conv_w": nrm(ks[3], (N_A, CONV_WIDTH, D_MODEL), CONV_WIDTH),
        "conv_out_w": nrm(ks[4], (N_A, D_MODEL, D_MODEL), D_MODEL),
        "kv_norm_g": 1.0 + 0.05 * jax.random.normal(ks[5], (D_MODEL,), f32),
        "kv_w": nrm(ks[6], (D_MODEL, 2 * D_MODEL), D_MODEL),
        "q_w": nrm(ks[7], (N_B, D_MODEL, D_MODEL), D_MODEL),
        "o_w": nrm(ks[8], (N_B, D_MODEL, D_MODEL), D_MODEL),
        "ffn_in_w": nrm(ks[9], (DEPTH, D_MODEL, 2 * D_FF), D_MODEL),
        "ffn_out_w": nrm(ks[10], (DEPTH, D_FF, D_MODEL), D_FF),
    }

def reference(x, norm_g, conv_in_w, conv_w, conv_out_w, kv_norm_g, kv_w, q_w, o_w,
              ffn_in_w, ffn_out_w):
    slopes = _alibi_slopes()
    shared = None
    for layer in range(DEPTH):
        g = norm_g[layer]
        xn = _rms_norm(x, g[0])
        if layer < N_A:
            mix = _short_conv(xn, conv_in_w[layer], conv_w[layer], conv_out_w[layer])
        else:
            if shared is None:
                shared = _shared_kv(x, kv_norm_g, kv_w)
            j = layer - N_A
            mix = _dilated_attention(xn, q_w[j], o_w[j], shared, slopes)
        x = x + _rms_norm(mix, g[1])
        ff = _swiglu(_rms_norm(x, g[2]), ffn_in_w[layer], ffn_out_w[layer])
        x = x + _rms_norm(ff, g[3])
    return x


_drawn_inputs = setup_inputs


def setup_inputs(seed=0):
    import zlib

    import numpy as np

    out = dict(_drawn_inputs(seed))
    spreads = {}
    factors = {}
    for name, (base, spread) in spreads.items():
        noise = np.random.default_rng([zlib.crc32(name.encode()), seed]).standard_normal(out[name].shape)
        drawn = base * np.exp(spread * noise) if base else spread * noise
        out[name] = __import__('jax').numpy.asarray(drawn.astype(out[name].dtype))
    for name, factor in factors.items():
        out[name] = (out[name] * factor).astype(out[name].dtype)
    return out
```

```python
from contextlib import ExitStack

import numpy as np

import concourse.bass as bass
from concourse import mybir

F32 = mybir.dt.float32
F32R = mybir.dt.float32r
BF16 = mybir.dt.bfloat16
F16 = mybir.dt.float16
I32 = mybir.dt.int32
ALU = mybir.AluOpType
ACT = mybir.ActivationFunctionType

P = 128
HALF = 512
EPS = 1e-6
MASKED = 1e30
DILATED_GROUPS = ((128, 1), (512, 4), (2048, 16))

RAW_RING = 2
SPLIT_RING = 3
CREDIT = 16

PHASES = ("norm0", "conv_in", "conv_out", "norm1", "ffn0", "norm2",
          "attn", "oturn", "oproj", "norm3", "ffn1", "norm4")


class Signal:

    def __init__(self, sem, per_phase):
        self.sem = sem
        self.start = {}
        total = CREDIT
        for ph in PHASES:
            self.start[ph] = total
            total += per_phase.get(ph, 0)

    def at(self, phase, count):
        return self.sem, count + self.start[phase]


def trunk(nc, x, norm_g, conv_in_w, conv_w, conv_out_w, kv_norm_g, kv_w, q_w, o_w,
          ffn_in_w, ffn_out_w, out):
    _, SEQ, D = x.shape
    TT = SEQ // P
    KT = D // P
    DFF = ffn_out_w.shape[1]
    FT = DFF // P
    GROUPS = FT // 2
    HD = 64
    PAIRS = D // P
    STEPS = 2 * TT
    CHUNK = KT * P
    assert SEQ == D == 1024 and FT % 2 == 0 and FT >= 4

    ffn_chunks = 3 * FT
    chunks = {"conv_in": 3 * KT, "conv_out": KT, "ffn0": ffn_chunks, "attn": 3 * PAIRS,
              "oproj": KT, "ffn1": ffn_chunks}
    chunk0 = {}
    total = 0
    for ph in PHASES:
        chunk0[ph] = total
        total += chunks.get(ph, 0)
    CHUNKS = total

    with ExitStack() as ctx:
        sem = lambda name: ctx.enter_context(nc.semaphore(name))

        def place(names):
            made = {}
            with ExitStack() as scope:
                for name, shape, dt in names:
                    made[name] = scope.enter_context(nc.sbuf_tensor(name, [P, *shape], dt))
            return made

        keep = lambda name, shape, dt=F32: ctx.enter_context(nc.sbuf_tensor(name, [P, *shape], dt))

        mix_conv = place([("mix_conv", [KT, SEQ], F32)])["mix_conv"]
        x_lo = keep("x_lo", [KT, SEQ], F32R)
        x_hi = keep("x_hi", [KT, SEQ], F32R)
        resid = keep("resid", [TT, D])
        raw = keep("raw", [RAW_RING, CHUNK])
        w_hi = keep("w_hi", [SPLIT_RING, CHUNK], F32R)
        w_lo = keep("w_lo", [SPLIT_RING, CHUNK], F32R)
        ident = keep("ident", [P])
        ones = keep("ones", [1])
        neg_half = keep("neg_half", [1])
        taps = keep("taps", [3, KT])
        gains = keep("gains", [3 * PAIRS + 2, KT])
        square1 = keep("square1", [TT])
        square2 = keep("square2", [TT])
        mean1 = keep("mean1", [TT])
        mean2 = keep("mean2", [TT])
        rstd1 = keep("rstd1", [TT])
        rstd2 = keep("rstd2", [TT])
        slope = keep("slope", [2])
        neg_max = keep("neg_max", [2])
        den = keep("den", [2])
        rden = keep("rden", [2])

        conv = place([("c_gate", [2, HALF], F32), ("u", [SEQ + 2], F32), ("y", [2, HALF], F32),
                      ("y_hi", [KT, SEQ], F32R), ("y_lo", [KT, SEQ], F32R)])
        ffn = place([("junk", [D], BF16),
                     ("xn", [2, D], F32), ("g_post", [D], F32), ("g_pre", [D], F32),
                     ("acc", [TT, D], F32), ("hid_hi", [2, SEQ], F32R), ("hid_lo", [2, SEQ], F32R),
                     ("hid", [2, HALF], F32), ("silu_gate", [2, HALF], F32)])
        dist_i = place([("dist_i", [SEQ], I32)])["dist_i"]
        att = place([("pt_hi", [2, SEQ], F32R), ("pt_lo", [2, SEQ], F32R),
                     ("q_hi", [SEQ], F32R), ("q_lo", [SEQ], F32R),
                     ("k_hi", [2, SEQ], F32R), ("k_lo", [2, SEQ], F32R),
                     ("v_split", [2, TT, 2, P], F32R),
                     ("dist", [SEQ], F16), ("neg_log", [SEQ], F32), ("bias", [SEQ], F32),
                     ("scores", [2, SEQ], F32), ("v_t", [HALF], F32), ("o_parts", [2, P], F32)])
        c_gate, u, y, y_hi, y_lo = (conv[n] for n in ("c_gate", "u", "y", "y_hi", "y_lo"))
        junk, xn, g_post, g_pre, acc = (ffn[n] for n in ("junk", "xn", "g_post", "g_pre", "acc"))
        hid_hi, hid_lo, hid, silu_gate = (ffn[n] for n in ("hid_hi", "hid_lo", "hid", "silu_gate"))

        psum = ctx.enter_context(nc.psum_tensor("banks", [P, 8, HALF], F32))
        bank = lambda b: psum[:, b, :]
        two_banks = lambda b: psum[:, b:b + 2, :].rearrange("p a c -> p (a c)")

        x_spill = nc.dram_tensor("x_spill", (TT, P, D), F32, kind="Internal").ap()

        raw_in = [sem(f"raw_in{i}") for i in range(RAW_RING)]
        x_in = [sem(f"x_in{t}") for t in range(TT)]
        consts_in = sem("consts_in")
        post_in, pre_in = sem("post_in"), sem("pre_in")
        held, held_sp = sem("held"), sem("held_sp")
        spilled, x_back, stored = sem("spilled"), sem("x_back"), sem("stored")

        def signal(name, **per_phase):
            return Signal(sem(name), per_phase)

        every_norm = {f"norm{i}": TT for i in range(5)}
        with_post = {f"norm{i}": TT for i in range(1, 5)}
        with_pre = {f"norm{i}": TT for i in range(4)}
        turned = {**with_pre, "oturn": TT}
        half_done = signal("half_done", conv_in=3 * KT, ffn0=2 * FT, ffn1=2 * FT, attn=3 * PAIRS)
        chunk_done = signal("chunk_done", **chunks)
        tok_done = signal("tok_done", conv_out=2 * (TT - 1), oproj=2 * (TT - 1),
                          ffn0=GROUPS * (2 * TT - 1), ffn1=GROUPS * (2 * TT - 1))
        xt_turned = signal("xt_turned", **turned)
        v_turned = signal("v_turned", attn=2 * PAIRS)
        s_done = signal("s_done", attn=STEPS * PAIRS)
        p_turned = signal("p_turned", attn=STEPS * PAIRS)
        pv_done = signal("pv_done", attn=STEPS * PAIRS)
        hi_ready = signal("hi_ready", **chunks)
        c_done = signal("c_done", conv_in=2 * KT)
        yh_done = signal("yh_done", conv_in=2 * KT)
        mix_done = signal("mix_done", conv_out=2 * TT, oproj=2 * TT)
        sq1_done = signal("sq1_done", **with_post)
        sq2_done = signal("sq2_done", **with_pre)
        xh_ready = signal("xh_ready", **turned)
        silu_done = signal("silu_done", ffn0=2 * FT, ffn1=2 * FT)
        hh_done = signal("hh_done", ffn0=2 * FT, ffn1=2 * FT)
        k_hi_done = signal("k_hi_done", attn=2 * PAIRS)
        q_hi_done = signal("q_hi_done", attn=2 * PAIRS)
        v_done = signal("v_done", attn=2 * PAIRS)
        vv_hi = signal("vv_hi", attn=2 * PAIRS)
        exp_done = signal("exp_done", attn=STEPS * PAIRS)
        ph_done = signal("ph_done", attn=STEPS * PAIRS)
        o_done = signal("o_done", attn=STEPS * PAIRS)
        lo_ready = signal("lo_ready", **chunks)
        u_done = signal("u_done", conv_in=2 * KT)
        tap_done = signal("tap_done", conv_in=6 * KT)
        ymul_done = signal("ymul_done", conv_in=2 * KT)
        yl_done = signal("yl_done", conv_in=2 * KT)
        scaled = signal("scaled", **with_post)
        x_new = signal("x_new", **with_post)
        xn_ready = signal("xn_ready", **with_pre)
        xl_ready = signal("xl_ready", **turned)
        hid_done = signal("hid_done", ffn0=2 * FT, ffn1=2 * FT)
        hl_done = signal("hl_done", ffn0=2 * FT, ffn1=2 * FT)
        add_done = signal("add_done", ffn0=GROUPS * 2 * TT, ffn1=GROUPS * 2 * TT)
        table_step = signal("table_step", norm0=1, attn=32)
        bias_ready = signal("bias_ready", attn=2 * PAIRS)
        slope_ready = signal("slope_ready", attn=1 + PAIRS)
        k_lo_done = signal("k_lo_done", attn=2 * PAIRS)
        q_lo_done = signal("q_lo_done", attn=2 * PAIRS)
        vv_lo = signal("vv_lo", attn=2 * PAIRS)
        max_done = signal("max_done", attn=STEPS * PAIRS)
        pl_done = signal("pl_done", attn=STEPS * PAIRS)
        rden_done = signal("rden_done", attn=STEPS * PAIRS)
        setup_step = signal("setup_step", norm0=4)
        gain_step = signal("gain_step", norm2=4)
        dist_ready = signal("dist_ready", attn=1)
        mean1_done = signal("mean1_done", **with_post)
        rstd1_done = signal("rstd1_done", **with_post)
        mean2_done = signal("mean2_done", **with_pre)
        rstd2_done = signal("rstd2_done", **with_pre)
        acc_zero = signal("acc_zero", ffn0=1, ffn1=1)
        w_scaled = signal("w_scaled", attn=chunks["attn"] + 2)
        o_ready = signal("o_ready", attn=STEPS * PAIRS)

        def grant(eng, *signals):
            for s in signals:
                eng.sem_inc(s.sem, CREDIT)

        tile_of = lambda a, t: a[:, :, t * P:(t + 1) * P]
        by_tile = lambda a: a.rearrange("p (k c) -> p k c", c=P)

        def mixed(phase, t):
            if phase == "norm1":
                return tile_of(mix_conv, t)
            return by_tile(acc[:, t, :])

        def row(g):
            return g.partition_broadcast(P)

        def turn_bank(ph, t):
            return 2 * (t % 2) + (4 * (t // (TT // 2)) if ph not in ("norm2", "oturn") else 0)

        def a_slot(n):
            return n % SPLIT_RING

        block = ctx.enter_context(nc.Block())

        RUN = 3
        PER_HALF = 3 * KT
        RUNS = 6 * PER_HALF // RUN
        slots = [3] * STEPS
        assert sum(slots) == RUNS
        ends = [sum(slots[:s + 1]) * RUN for s in range(STEPS)]
        ends_in = [next(s for s in range(STEPS) if ends[s] >= (j + 1) * PER_HALF) for j in range(6)]
        SCORE, PROB, OUT, VTURN, PROJ = 0, 2, 4, 5, 6

        @block.sync
        def _(sp):
            def column_chunk(w, col):
                return w.rearrange("(k p) n -> p k n", p=P)[:, :, bass.ds(col, P)]

            def load(n, src):
                fixed, moving = n
                s = fixed % RAW_RING
                sp.wait_ge(lo_ready.sem, moving + (fixed - RAW_RING + 1 + CREDIT))
                if not isinstance(moving, int):
                    sp.sem_inc(held_sp, 1)
                sp.dma_start(raw[:, s, :].rearrange("p (k c) -> p k c", c=src.shape[-1])
                             if len(src.shape) == 3 else raw[:, s, :], src).then_inc(raw_in[s], 16)

            def load_two_row_blocks(ph, w):
                for c in range(KT):
                    half, q = c // (KT // 2), c % (KT // 2)
                    load((chunk0[ph] + c, 0),
                         w.rearrange("(k p) n -> p k n", p=P)[:, 2 * q:2 * q + 2,
                                                             half * HALF:(half + 1) * HALF])

            def load_ffn(ph, layer):
                w_in, w_out = ffn_in_w[layer], ffn_out_w[layer]
                base = chunk0[ph]
                for j in range(2):
                    for part in range(2):
                        load((base + 2 * j + part, 0), column_chunk(w_in, part * DFF + j * P))
                with sp.Fori(0, GROUPS - 1) as g:
                    for pos, (what, j) in enumerate((("in", 0), ("in", 0), ("out", 0), ("out", 1),
                                                     ("in", 1), ("in", 1))):
                        n = (base + 4 + pos, g * 6)
                        if what == "in":
                            part = pos % 2
                            load(n, column_chunk(w_in, g * (2 * P) + (2 * P + j * P + part * DFF)))
                        else:
                            load(n, w_out[bass.ds(g * (2 * P) + j * P, P), :])
                for j in range(2):
                    load((base + ffn_chunks - 2 + j, 0),
                         w_out[(FT - 2 + j) * P:(FT - 1 + j) * P, :])

            with nc.allow_non_contiguous_dma("per-feature gains and taps"):
                sp.dma_start(g_pre[:], row(norm_g[0, 0])).then_inc(pre_in, 16)
                for t in range(TT):
                    sp.dma_start(resid[:, t, :], x[0, t * P:(t + 1) * P, :]).then_inc(x_in[t], 16)
                for j in range(3):
                    sp.dma_start(taps[:, j, :], conv_w[0, j].rearrange("(k p) -> p k", p=P)) \
                        .then_inc(consts_in, 16)
                sp.dma_start(gains[:, 2, :], norm_g[1, 0].rearrange("(k p) -> p k", p=P)) \
                    .then_inc(consts_in, 16)
                sp.dma_start(gains[:, 0, :], kv_norm_g.rearrange("(k p) -> p k", p=P)) \
                    .then_inc(consts_in, 16)

            with sp.Fori(0, KT // 2) as g:
                for pos in range(6):
                    f, part = pos // 3, (1, 2, 0)[pos % 3]
                    load((pos, g * 6), column_chunk(conv_in_w[0], g * (2 * P) + (part * D + f * P)))
            load_two_row_blocks("conv_out", conv_out_w[0])
            load_ffn("ffn0", 0)
            with sp.Fori(0, PAIRS // 2) as g:
                for pos in range(6):
                    col = g * (2 * P) + (pos // 3) * P
                    src = (kv_w, kv_w, q_w[0])[pos % 3]
                    load((chunk0["attn"] + pos, g * 6),
                         column_chunk(src, col + (D if pos % 3 == 1 else 0)))
            load_two_row_blocks("oproj", o_w[0])
            load_ffn("ffn1", 1)
            for t in range(TT):
                sp.wait_ge(*x_new.at("norm4", t + 1))
                sp.dma_start(out[0, t * P:(t + 1) * P, :], resid[:, t, :]).then_inc(stored, 16)
            sp.wait_ge(stored, 16 * TT)

        @block.tensor
        def _(pe):
            grant(pe, half_done, chunk_done, tok_done, xt_turned, v_turned, s_done, p_turned,
                  pv_done)

            def weights(n, ph, moving=0):
                pe.wait_ge(*lo_ready.at(ph, moving + n))

            def feature_product(slot, banks, free, half_count, ph):
                wk = lambda w, k: w[:, slot, k * P:(k + 1) * P]
                for h in range(2):
                    if free is not None:
                        free(h)
                    passes = [(w, a, k) for w, a in ((w_hi, x_hi), (w_hi, x_lo), (w_lo, x_hi))
                              for k in range(KT)]
                    for i, (w, a, k) in enumerate(passes):
                        mm = pe.matmul(bank(banks + h), wk(w, k), a[:, k, h * HALF:(h + 1) * HALF],
                                       start=(i == 0), stop=(i == len(passes) - 1))
                    mm.then_inc((chunk_done if h else half_done).sem, 1)

            def turn_tile(ph, t, src):
                pe.wait_ge(*xl_ready.at(ph, t - 1))
                b = turn_bank(ph, t)
                for k in range(KT):
                    mm = pe.transpose(psum[:, b + k // 4, (k % 4) * P:(k % 4 + 1) * P],
                                      src[:, k * P:(k + 1) * P], ident[:])
                mm.then_inc(xt_turned.sem, 1)

            def norm(ph):
                for t in range(TT):
                    pe.wait_ge(*xn_ready.at(ph, t + 1))
                    if ph in ("norm1", "norm3"):
                        pe.wait_ge(*mix_done.at({"norm1": "conv_out", "norm3": "oproj"}[ph],
                                                TT + turn_bank(ph, t) + 2))
                    turn_tile(ph, t, xn[:, t % 2, :])

            def token_product(ph, a_hi, a_lo):
                for c in range(KT):
                    half, q = c // (KT // 2), c % (KT // 2)
                    last = q == KT // 2 - 1
                    weights(c + 1, ph)
                    slot = a_slot(chunk0[ph] + c)
                    for t in range(TT):
                        if half and q == 0:
                            pe.wait_ge(*mix_done.at(ph, t + 1))
                        passes = [(a, w, k) for a, w in ((a_hi, w_hi), (a_hi, w_lo), (a_lo, w_hi))
                                  for k in range(2)]
                        for i, (a, w, k) in enumerate(passes):
                            mm = pe.matmul(bank(t), a[:, 2 * q + k, t * P:(t + 1) * P],
                                           w[:, slot, k * HALF:(k + 1) * HALF],
                                           start=(q == 0 and i == 0),
                                           stop=(last and i == len(passes) - 1))
                        if t == TT - 1:
                            mm.then_inc(chunk_done.sem, 1)
                        elif last:
                            mm.then_inc(tok_done.sem, 1)

            pe.wait_ge(*setup_step.at("norm0", 4))
            norm("norm0")

            pe.wait_ge(*xl_ready.at("norm0", TT))
            with pe.Fori(0, KT // 2) as g:
                for pos in range(6):
                    f = pos // 3
                    weights(pos + 1, "conv_in", g * 6)

                    def free(h, pos=pos, f=f):
                        if pos % 3 == 0:
                            pe.wait_ge(*u_done.at("conv_in", g * 4 + (2 * f - 1 + h)))
                        elif pos % 3 == 1:
                            pe.wait_ge(*ymul_done.at("conv_in", g * 4 + (2 * f - 1 + h)))
                        else:
                            pe.wait_ge(*c_done.at("conv_in", g * 4 + (2 * f + 1 + h)))

                    feature_product(a_slot(pos), 2 * (pos % 2), free, None, "conv_in")

            pe.wait_ge(*yl_done.at("conv_in", 2 * KT))
            token_product("conv_out", y_hi, y_lo)
            norm("norm1")

            def ffn_layer(ph, norm_ph):
                base = chunk0[ph]
                pe.wait_ge(*xl_ready.at(norm_ph, TT))

                def in_product(n, moving, j, part, tiles):
                    weights(n - base + 1, ph, moving)

                    def free(h):
                        pe.wait_ge(*(hid_done if part else silu_done).at(ph, tiles + (2 * j - 1 + h)))

                    feature_product(a_slot(n), 2 * part, free, None, ph)

                def out_product(n, moving, g):
                    weights(n - base + 2, ph, moving)
                    pe.wait_ge(*hl_done.at(ph, g * 4 + 4))
                    for o in range(2 * TT):
                        t, h = o // 2, o % 2
                        pe.wait_ge(*add_done.at(ph, g * (2 * TT) + (o - 3)))
                        passes = [(a, w, j) for a, w in ((hid_hi, w_hi), (hid_hi, w_lo),
                                                        (hid_lo, w_hi)) for j in range(2)]
                        for i, (a, w, j) in enumerate(passes):
                            mm = pe.matmul(bank(4 + o % 4), a[:, j, t * P:(t + 1) * P],
                                           w[:, a_slot(n + j), h * HALF:(h + 1) * HALF],
                                           start=(i == 0), stop=(i == len(passes) - 1))
                        if o < 2 * TT - 1:
                            mm.then_inc(tok_done.sem, 1)
                        else:
                            mm.then_inc(chunk_done.sem, 2)

                for j in range(2):
                    for part in range(2):
                        in_product(base + 2 * j + part, 0, j, part, 0)
                with pe.Fori(0, GROUPS - 1) as g:
                    tiles = g * 4 + 4
                    in_product(base + 4, g * 6, 0, 0, tiles)
                    in_product(base + 5, g * 6, 0, 1, tiles)
                    out_product(base + 6, g * 6, g)
                    in_product(base + 8, g * 6, 1, 0, tiles)
                    in_product(base + 9, g * 6, 1, 1, tiles)
                out_product(base + ffn_chunks - 2, 0, GROUPS - 1)

            ffn_layer("ffn0", "norm1")
            norm("norm2")

            def project(r, i):
                moving, fixed = r
                j, i = i // PER_HALF, i % PER_HALF
                part, h = j // 2, j % 2
                c = 3 * fixed + part
                if i == 0:
                    if h == 0:
                        pe.wait_ge(*lo_ready.at("attn", moving * 3 + (c + 1)))
                    before = moving * 2 + (2 * fixed + h)
                    if part == 0:
                        pe.wait_ge(*q_lo_done.at("attn", before - 1))
                    elif part == 1:
                        pe.wait_ge(*k_lo_done.at("attn", before + 1))
                    else:
                        pe.wait_ge(*v_done.at("attn", before + 1))
                n, k = i // KT, i % KT
                w, a = ((w_hi, x_hi), (w_hi, x_lo), (w_lo, x_hi))[n]
                mm = pe.matmul(bank(PROJ + h), w[:, a_slot(chunk0["attn"] + c), k * P:(k + 1) * P],
                               a[:, k, h * HALF:(h + 1) * HALF],
                               start=(i == 0), stop=(i == PER_HALF - 1))
                if i == PER_HALF - 1:
                    mm.then_inc((chunk_done if h else half_done).sem, 1)

            def turn_values(r, h):
                moving, fixed = r
                before = moving * 2 + (2 * fixed + h)
                pe.wait_ge(*v_done.at("attn", before + 1))
                pe.wait_ge(*vv_lo.at("attn", before))
                for j in range(4):
                    mm = pe.transpose(psum[:, VTURN, j * P:(j + 1) * P],
                                      att["v_t"][:, j * P:(j + 1) * P], ident[:])
                mm.then_inc(v_turned.sem, 1)

            def attend(a, after):
                moving, fixed = a
                parity = fixed % 2
                steps = moving * STEPS + fixed * STEPS
                nxt = (moving, fixed + 1)

                def scores(s):
                    pair, s_in = fixed + s // STEPS, s % STEPS
                    e, i = s_in // TT, s_in % TT
                    rows = slice(HD * e, HD * e + HD)
                    n_keys = (i + 1) * P
                    pe.wait_ge(*max_done.at("attn", steps + s))
                    halves = moving * 2 + (2 * pair + 1 + i // 4)
                    pe.wait_ge(*q_lo_done.at("attn", halves))
                    for lo in range(0, n_keys, HALF):
                        hi = min(lo + HALF, n_keys)
                        passes = (("q_hi", "k_hi"), ("q_hi", "k_lo"), ("q_lo", "k_hi"))
                        for n, (q, k) in enumerate(passes):
                            mm = pe.matmul(psum[:, SCORE + lo // HALF, 0:hi - lo],
                                           att[q][rows, i * P:(i + 1) * P],
                                           att[k][rows, pair % 2, lo:hi],
                                           start=(n == 0), stop=(n == 2))
                    mm.then_inc(s_done.sem, 1)

                def turn_probs(s):
                    i = s % TT
                    pe.wait_ge(*exp_done.at("attn", steps + (s + 1)))
                    pe.wait_ge(*pl_done.at("attn", steps + s))
                    for j in range(i + 1):
                        mm = pe.transpose(psum[:, PROB + j // 4, (j % 4) * P:(j % 4 + 1) * P],
                                          att["scores"][:, s % 2, j * P:(j + 1) * P], ident[:])
                    mm.then_inc(p_turned.sem, 1)

                def outputs(s):
                    e, i = s // TT, s % TT
                    pe.wait_ge(*pl_done.at("attn", steps + (s + 1)))
                    pe.wait_ge(*vv_lo.at("attn", moving * 2 + (2 * fixed + 1 + i // 4)))
                    pe.wait_ge(*o_done.at("attn", steps + s))
                    for n in range(2 * (i + 1)):
                        j = n % (i + 1)
                        p = att["pt_hi" if n <= i else "pt_lo"]
                        mm = pe.matmul(psum[:, OUT, 0:P], p[:, s % 2, j * P:(j + 1) * P],
                                       att["v_split"][:, parity, j, e, :],
                                       start=(n == 0), stop=(n == 2 * i + 1))
                    mm.then_inc(pv_done.sem, 1)

                for s in range(STEPS):
                    runs = slots[s] if after else 0
                    first = ends[s] - slots[s] * RUN

                    def fill(r0, r1):
                        for i in range(first + r0 * RUN, first + r1 * RUN):
                            project(nxt, i)

                    third = (runs + 2) // 3
                    if s + 1 < STEPS or after:
                        scores(s + 1)
                    fill(0, min(third, runs))
                    turn_probs(s)
                    fill(min(third, runs), min(2 * third, runs))
                    if s >= 1:
                        outputs(s - 1)
                    if after and s in (ends_in[2] + 2, ends_in[3] + 2):
                        turn_values(nxt, 0 if s == ends_in[2] + 2 else 1)
                    fill(min(2 * third, runs), runs)
                outputs(STEPS - 1)

            pe.wait_ge(*xl_ready.at("norm2", TT))
            for i in range(RUNS * RUN):
                if i in (3 * PER_HALF + KT, 4 * PER_HALF + KT):
                    turn_values((0, 0), i // PER_HALF - 3)
                project((0, 0), i)
            pe.wait_ge(*q_lo_done.at("attn", 1))
            for n, (q, k) in enumerate((("q_hi", "k_hi"), ("q_hi", "k_lo"), ("q_lo", "k_hi"))):
                mm = pe.matmul(psum[:, SCORE, 0:P], att[q][0:HD, 0:P], att[k][0:HD, 0, 0:P],
                               start=(n == 0), stop=(n == 2))
            mm.then_inc(s_done.sem, 1)
            with pe.Fori(0, PAIRS // 2 - 1) as g:
                for pp in range(2):
                    attend((g * 2, pp), True)
            attend((0, PAIRS - 2), True)
            attend((0, PAIRS - 1), False)

            for t in range(TT):
                pe.wait_ge(*o_ready.at("attn", STEPS * PAIRS - TT + t + 1))
                if t == 0:
                    pe.wait_ge(*pl_done.at("attn", STEPS * PAIRS))
                turn_tile("oturn", t, resid[:, t, :])
            pe.wait_ge(*xl_ready.at("oturn", TT))
            token_product("oproj", x_hi, x_lo)
            norm("norm3")
            ffn_layer("ffn1", "norm3")

        @block.scalar
        def _(act):
            grant(act, hi_ready, c_done, yh_done, mix_done, sq1_done, sq2_done, xh_ready,
                  silu_done, hh_done, k_hi_done, q_hi_done, v_done, vv_hi, exp_done, ph_done, o_done)

            def prepare(n, moving=0):
                if n >= CHUNKS:
                    return
                s = n % RAW_RING
                if chunk0["attn"] <= n < chunk0["oproj"] + 2:
                    act.wait_ge(w_scaled.sem, moving + (n - chunk0["attn"] + 1
                                                        + w_scaled.start["attn"]))
                elif isinstance(moving, int):
                    act.wait_ge(raw_in[s], 16 * (n // RAW_RING + 1))
                else:
                    act.wait_ge(raw_in[s], moving * (16 // RAW_RING) + 16 * (n // RAW_RING + 1))
                act.wait_ge(chunk_done.sem, moving + (n - SPLIT_RING + 1 + CREDIT))
                act.copy(w_hi[:, n % SPLIT_RING, :], raw[:, s, :]).then_inc(hi_ready.sem, 1)

            def product(ph, h, a_count, n_count):
                if h == 0:
                    act.wait_ge(*half_done.at(ph, a_count))
                else:
                    act.wait_ge(*chunk_done.at(ph, n_count))

            def high_part(ph, t):
                act.wait_ge(*xt_turned.at(ph, t + 1))
                act.copy(tile_of(x_hi, t), by_tile(two_banks(turn_bank(ph, t)))) \
                    .then_inc(xh_ready.sem, 1)

            def norm(ph, late=CHUNKS):
                post, pre = ph != "norm0", ph != "norm4"
                for i in range(TT + 2):
                    if i == TT:
                        prepare(late)
                    if post and i < TT:
                        if ph in ("norm1", "norm3"):
                            act.wait_ge(*mix_done.at({"norm1": "conv_out", "norm3": "oproj"}[ph],
                                 TT + i + 1))
                        else:
                            act.wait_ge(*add_done.at({"norm2": "ffn0", "norm4": "ffn1"}[ph],
                                 (GROUPS - 1) * 2 * TT + 2 * i + 2))
                        if pre and i >= 2:
                            act.wait_ge(*sq2_done.at(ph, i - 1))
                        elif i >= 1:
                            act.wait_ge(*sq1_done.at(ph, i))
                        act.activation(by_tile(junk[:]), mixed(ph, i), ACT.Square,
                                       accum_out=square1[:, i:i + 1]).then_inc(sq1_done.sem, 1)
                    t = i - 1 if post else i
                    if pre and 0 <= t < TT:
                        if post:
                            act.wait_ge(*x_new.at(ph, t + 1))
                        else:
                            act.wait_ge(x_in[t], 16)
                        if not post:
                            act.wait_ge(*sq2_done.at(ph, t))
                        elif i < TT:
                            act.wait_ge(*sq1_done.at(ph, i + 1))
                        else:
                            act.wait_ge(*sq2_done.at(ph, t))
                        act.activation(junk[:], resid[:, t, :], ACT.Square,
                                       accum_out=square2[:, t:t + 1]).then_inc(sq2_done.sem, 1)
                    if pre and i >= 2:
                        high_part(ph, i - 2)

            def token_product(ph):
                for c in range(KT):
                    prepare(chunk0[ph] + c + 2)
                    half, q = c // (KT // 2), c % (KT // 2)
                    if q < KT // 2 - 1:
                        continue
                    for t in range(TT):
                        if t < TT - 1:
                            act.wait_ge(*tok_done.at(ph, half * (TT - 1) + t + 1))
                        else:
                            act.wait_ge(*chunk_done.at(ph, c + 1))
                        if ph == "conv_out":
                            dst = mix_conv[:, 4 * half:4 * half + 4, t * P:(t + 1) * P]
                        else:
                            dst = by_tile(acc[:, t, half * HALF:(half + 1) * HALF])
                        act.copy(dst, by_tile(bank(t))).then_inc(mix_done.sem, 1)

            prepare(0)
            prepare(1)
            norm("norm0")
            with act.Fori(0, KT // 2) as g:
                for pos in range(6):
                    f = pos // 3
                    prepare(pos + 2, g * 6)
                    for h in range(2):
                        if pos % 3 == 0:
                            product("conv_in", h, g * 6 + (pos + 1), g * 6 + (pos + 1))
                            act.wait_ge(*u_done.at("conv_in", g * 4 + (2 * f - 1 + h)))
                            act.copy(c_gate[:, h, :], bank(2 * (pos % 2) + h)) \
                                .then_inc(c_done.sem, 1)
                        elif pos % 3 == 2:
                            act.wait_ge(*ymul_done.at("conv_in", g * 4 + (2 * f + 1 + h)))
                            act.copy(y_hi[:, g * 2 + f, h * HALF:(h + 1) * HALF], y[:, h, :]) \
                                .then_inc(yh_done.sem, 1)
            token_product("conv_out")
            act.dma_start(g_post[:], row(norm_g[0, 1])).then_inc(post_in, 16)
            act.dma_start(g_pre[:], row(norm_g[0, 2])).then_inc(pre_in, 16)
            norm("norm1")

            def ffn_layer(ph):
                base = chunk0[ph]

                def silu(n, moving, j, tiles):
                    for h in range(2):
                        product(ph, h, tiles + (2 * j + 1), moving + (n + 1))
                        act.wait_ge(*hid_done.at(ph, tiles + (2 * j - 1 + h)))
                        act.activation(silu_gate[:, h, :], bank(h), ACT.Silu) \
                            .then_inc(silu_done.sem, 1)

                def hidden_high(j, tiles):
                    for h in range(2):
                        act.wait_ge(*hid_done.at(ph, tiles + (2 * j + 1 + h)))
                        act.copy(hid_hi[:, j, h * HALF:(h + 1) * HALF], hid[:, h, :]) \
                            .then_inc(hh_done.sem, 1)

                act.wait_ge(*x_new.at({"ffn0": "norm1", "ffn1": "norm3"}[ph], TT))
                act.dma_start(g_post[:], row(norm_g[0 if ph == "ffn0" else 1, 3])) \
                    .then_inc(post_in, 16)
                for j in range(2):
                    prepare(base + 2 * j + 2)
                    silu(2 * j, 0, j, 0)
                    prepare(base + 2 * j + 3)
                    hidden_high(j, 0)
                with act.Fori(0, GROUPS - 1) as g:
                    tiles = g * 4 + 4
                    prepare(base + 6, g * 6)
                    silu(4, g * 6, 0, tiles)
                    prepare(base + 7, g * 6)
                    prepare(base + 8, g * 6)
                    act.wait_ge(*chunk_done.at(ph, g * 6 + 8))
                    prepare(base + 9, g * 6)
                    hidden_high(0, tiles)
                    prepare(base + 10, g * 6)
                    silu(8, g * 6, 1, tiles)
                    prepare(base + 11, g * 6)
                    hidden_high(1, tiles)
                prepare(base + ffn_chunks)

            ffn_layer("ffn0")
            norm("norm2", chunk0["attn"] + 1)
            act.dma_start(x_spill.rearrange("t p d -> p t d"), resid[:]).then_inc(spilled, 16)

            def project(r, j):
                moving, fixed = r
                part, h = j // 2, j % 2
                cols = slice(h * HALF, (h + 1) * HALF)
                product("attn", h, moving * 3 + (3 * fixed + part + 1),
                        moving * 3 + (3 * fixed + part + 1))
                if part == 0:
                    act.copy(att["k_hi"][:, fixed % 2, cols], bank(PROJ + h)) \
                        .then_inc(k_hi_done.sem, 1)
                elif part == 1:
                    act.wait_ge(*v_turned.at("attn", moving * 2 + (2 * fixed + h)))
                    act.copy(att["v_t"][:], bank(PROJ + h)).then_inc(v_done.sem, 1)
                else:
                    act.wait_ge(*s_done.at("attn", moving * STEPS
                                           + (fixed * STEPS - (1 - h) * TT // 2)))
                    act.activation(att["q_hi"][:, cols], bank(PROJ + h), ACT.Copy,
                                   scale=-float(HD) ** -0.5).then_inc(q_hi_done.sem, 1)

            def values_high(r, h):
                moving, fixed = r
                act.wait_ge(*v_turned.at("attn", moving * 2 + (2 * fixed + h + 1)))
                act.copy(att["v_split"][:, fixed % 2, 4 * h:4 * h + 4, :, 0:HD],
                         bank(VTURN).rearrange("p (j e d) -> p j e d", e=2, d=HD)) \
                    .then_inc(vv_hi.sem, 1)

            def attend(a, after):
                moving, fixed = a
                steps = moving * STEPS + fixed * STEPS
                nxt = (moving, fixed + 1)
                chunk = lambda c: prepare(chunk0["attn"] + 3 * (fixed + 1) + c,
                                          moving if isinstance(moving, int) else moving * 3)

                def probs_high(s):
                    n = (s % TT + 1) * P
                    act.wait_ge(*p_turned.at("attn", steps + (s + 1)))
                    act.wait_ge(*pv_done.at("attn", steps + (s - 1)))
                    act.copy(att["pt_hi"][:, s % 2, 0:n], two_banks(PROB)[:, 0:n]) \
                        .then_inc(ph_done.sem, 1)

                def outputs(s):
                    act.wait_ge(*pv_done.at("attn", steps + (s + 1)))
                    act.wait_ge(*rden_done.at("attn", steps + (s + 1)))
                    act.wait_ge(*o_ready.at("attn", steps + (s - 1)))
                    act.activation(att["o_parts"][:, s % 2, :], psum[:, OUT, 0:P],
                                   ACT.Copy, scale=rden[:, s % 2:s % 2 + 1]) \
                        .then_inc(o_done.sem, 1)

                for s in range(STEPS):
                    if s + 1 < STEPS or after:
                        exponentials(steps, s + 1)
                    probs_high(s)
                    if s >= 1:
                        outputs(s - 1)
                    if not after:
                        continue
                    for c, step in enumerate((1, ends_in[1] + 1, ends_in[3] + 1)):
                        if s == step:
                            chunk(2 + c)
                    for j in range(6):
                        if s == min(ends_in[j] + 1, STEPS - 1):
                            project(nxt, j)
                    for h in range(2):
                        if s == ends_in[2 + h] + 3:
                            values_high(nxt, h)
                outputs(STEPS - 1)

            def exponentials(steps, s):
                n = (s % TT + 1) * P
                act.wait_ge(*max_done.at("attn", steps + (s + 1)))
                act.wait_ge(*rden_done.at("attn", steps + (s - 1)))
                act.activation(att["scores"][:, s % 2, 0:n], att["scores"][:, s % 2, 0:n],
                               ACT.Exp, bias=neg_max[:, s % 2:s % 2 + 1], scale=-1.0,
                               accum_out=den[:, s % 2:s % 2 + 1]).then_inc(exp_done.sem, 1)

            prepare(chunk0["attn"] + 2)
            for j in range(6):
                project((0, 0), j)
                if j in (3, 4):
                    values_high((0, 0), j - 3)
                if j in (1, 3):
                    prepare(chunk0["attn"] + 3 + j // 2)
            exponentials(0, 0)
            with act.Fori(0, PAIRS // 2 - 1) as g:
                for pp in range(2):
                    attend((g * 2, pp), True)
            attend((0, PAIRS - 2), True)
            attend((0, PAIRS - 1), False)

            for t in range(TT):
                high_part("oturn", t)
            act.wait_ge(*xl_ready.at("oturn", TT))
            act.wait_ge(spilled, 16)
            act.dma_start(resid[:], x_spill.rearrange("t p d -> p t d")).then_inc(x_back, 16)
            act.dma_start(g_post[:], row(norm_g[1, 1])).then_inc(post_in, 16)
            act.dma_start(g_pre[:], row(norm_g[1, 2])).then_inc(pre_in, 16)
            token_product("oproj")
            norm("norm3")
            ffn_layer("ffn1")
            norm("norm4")

        @block.vector
        def _(dve):
            grant(dve, lo_ready, u_done, tap_done, ymul_done, yl_done, scaled, x_new, xn_ready,
                  xl_ready, hid_done, hl_done, add_done, table_step, bias_ready, slope_ready,
                  k_lo_done, q_lo_done, vv_lo, max_done, pl_done, rden_done)
            f32 = lambda a: a.bitcast(F32)

            def prepare(n, moving=0):
                if n >= CHUNKS:
                    return
                dve.wait_ge(hi_ready.sem, moving + (n + 1 + CREDIT))
                dve.tensor_tensor(w_lo[:, n % SPLIT_RING, :], raw[:, n % RAW_RING, :],
                                  f32(w_hi[:, n % SPLIT_RING, :]), ALU.subtract) \
                   .then_inc(lo_ready.sem, 1)

            def product(ph, h, a_count, n_count):
                if h == 0:
                    dve.wait_ge(*half_done.at(ph, a_count))
                else:
                    dve.wait_ge(*chunk_done.at(ph, n_count))

            def low_part(ph, t):
                dve.wait_ge(*xh_ready.at(ph, t + 1))
                dve.tensor_tensor(tile_of(x_lo, t), by_tile(two_banks(turn_bank(ph, t))),
                                  f32(tile_of(x_hi, t)), ALU.subtract).then_inc(xl_ready.sem, 1)

            posts = {"norm1": 1, "norm2": 2, "norm3": 3, "norm4": 4}
            pres = {"norm0": 1, "norm1": 2, "norm3": 3}

            def norm(ph, late=CHUNKS):
                post, pre = ph != "norm0", ph != "norm4"
                if post:
                    dve.wait_ge(post_in, 16 * posts[ph])
                if ph in pres:
                    dve.wait_ge(pre_in, 16 * pres[ph])
                if ph == "norm3":
                    dve.wait_ge(x_back, 16)
                for i in range(TT + 2):
                    if i == TT:
                        prepare(late)
                    if post and i < TT:
                        m = mixed(ph, i)
                        dve.wait_ge(*rstd1_done.at(ph, i + 1))
                        dve.scalar_tensor_tensor(out=m, in0=m, scalar=rstd1[:, i:i + 1],
                                                 in1=by_tile(g_post[:]), op0=ALU.mult,
                                                 op1=ALU.mult).then_inc(scaled.sem, 1)
                        dve.wait_ge(*scaled.at(ph, i + 1))
                        dve.tensor_tensor(by_tile(resid[:, i, :]), by_tile(resid[:, i, :]), m,
                                          ALU.add).then_inc(x_new.sem, 1)
                    t = i - 1 if post else i
                    if pre and 0 <= t < TT:
                        dve.wait_ge(*rstd2_done.at(ph, t + 1))
                        dve.wait_ge(*xt_turned.at(ph, t - 1))
                        if ph in pres:
                            ins = dve.scalar_tensor_tensor(out=xn[:, t % 2, :], in0=resid[:, t, :],
                                                           scalar=rstd2[:, t:t + 1], in1=g_pre[:],
                                                           op0=ALU.mult, op1=ALU.mult)
                        else:
                            ins = dve.tensor_scalar(xn[:, t % 2, :], resid[:, t, :],
                                                    rstd2[:, t:t + 1], None, ALU.mult)
                        ins.then_inc(xn_ready.sem, 1)
                    if pre and i >= 2:
                        low_part(ph, i - 2)

            def token_product(ph):
                for c in range(KT):
                    prepare(chunk0[ph] + c + 2)

            prepare(0)
            prepare(1)
            norm("norm0")
            dve.wait_ge(*xt_turned.at("norm0", TT))
            dve.memset(u[:, 0:2], 0.0).then_inc(table_step.sem, 1)
            dve.wait_ge(consts_in, 16 * 5)
            dve.wait_ge(*table_step.at("conv_in", 0))
            with dve.Fori(0, KT // 2) as g:
                for pos in range(6):
                    f = pos // 3
                    prepare(pos + 2, g * 6)
                    tap = lambda j: taps[:, j, bass.ds(g * 2 + f, 1)]
                    for h in range(2):
                        cols = slice(h * HALF, (h + 1) * HALF)
                        count = g * 4 + (2 * f + 1 + h)
                        if pos % 3 == 1:
                            dve.wait_ge(*c_done.at("conv_in", count))
                            product("conv_in", h, g * 6 + (pos + 1), g * 6 + (pos + 1))
                            dve.tensor_tensor(u[:, h * HALF + 2:(h + 1) * HALF + 2],
                                              c_gate[:, h, :], bank(2 * (pos % 2) + h), ALU.mult) \
                               .then_inc(u_done.sem, 1)
                            dve.wait_ge(*u_done.at("conv_in", count))
                            dve.wait_ge(*yh_done.at("conv_in", g * 4 + (2 * f - 1 + h)))
                            for j in range(3):
                                ux = u[:, h * HALF + j:(h + 1) * HALF + j]
                                if j == 0:
                                    ins = dve.tensor_scalar(y[:, h, :], ux, tap(0), None, ALU.mult)
                                else:
                                    dve.wait_ge(*tap_done.at("conv_in", g * 12 + (6 * f + 3 * h + j)))
                                    ins = dve.scalar_tensor_tensor(
                                        out=y[:, h, :], in0=ux, scalar=tap(j), in1=y[:, h, :],
                                        op0=ALU.mult, op1=ALU.add)
                                ins.then_inc(tap_done.sem, 1)
                        elif pos % 3 == 2:
                            product("conv_in", h, g * 6 + (pos + 1), g * 6 + (pos + 1))
                            dve.wait_ge(*tap_done.at("conv_in", g * 12 + (6 * f + 3 * h + 3)))
                            dve.tensor_tensor(y[:, h, :], y[:, h, :], bank(2 * (pos % 2) + h),
                                              ALU.mult).then_inc(ymul_done.sem, 1)
                    if pos % 3 == 2:
                        for h in range(2):
                            cols = slice(h * HALF, (h + 1) * HALF)
                            dve.wait_ge(*yh_done.at("conv_in", g * 4 + (2 * f + 1 + h)))
                            dve.tensor_tensor(y_lo[:, g * 2 + f, cols], y[:, h, :],
                                              f32(y_hi[:, g * 2 + f, cols]), ALU.subtract) \
                               .then_inc(yl_done.sem, 1)
            token_product("conv_out")
            norm("norm1")

            def ffn_layer(ph):
                base = chunk0[ph]

                def hidden(n, moving, j, tiles):
                    for h in range(2):
                        product(ph, h, tiles + (2 * j + 2), moving + (n + 1))
                        dve.wait_ge(*silu_done.at(ph, tiles + (2 * j + 1 + h)))
                        dve.wait_ge(*hl_done.at(ph, tiles + (2 * j - 1 + h)))
                        dve.tensor_tensor(hid[:, h, :], silu_gate[:, h, :], bank(2 + h),
                                          ALU.mult).then_inc(hid_done.sem, 1)

                def hidden_low(j, tiles):
                    for h in range(2):
                        cols = slice(h * HALF, (h + 1) * HALF)
                        dve.wait_ge(*hh_done.at(ph, tiles + (2 * j + 1 + h)))
                        dve.tensor_tensor(hid_lo[:, j, cols], hid[:, h, :],
                                          f32(hid_hi[:, j, cols]), ALU.subtract) \
                           .then_inc(hl_done.sem, 1)

                def accumulate(moving, g):
                    for o in range(2 * TT):
                        t, h = o // 2, o % 2
                        if o < 2 * TT - 1:
                            dve.wait_ge(*tok_done.at(ph, g * (2 * TT - 1) + (o + 1)))
                        else:
                            dve.wait_ge(*chunk_done.at(ph, moving))
                        dve.wait_ge(*add_done.at(ph, g * (2 * TT) + (o - 2 * TT + 1)))
                        a = acc[:, t, h * HALF:(h + 1) * HALF]
                        dve.tensor_tensor(a, a, bank(4 + o % 4), ALU.add) \
                           .then_inc(add_done.sem, 1)

                for j in range(2):
                    prepare(base + 2 * j + 2)
                    prepare(base + 2 * j + 3)
                    hidden(2 * j + 1, 0, j, 0)
                    hidden_low(j, 0)
                dve.wait_ge(*acc_zero.at(ph, 1))
                with dve.Fori(0, GROUPS - 1) as g:
                    tiles = g * 4 + 4
                    prepare(base + 6, g * 6)
                    prepare(base + 7, g * 6)
                    hidden(5, g * 6, 0, tiles)
                    prepare(base + 8, g * 6)
                    accumulate(g * 6 + 8, g)
                    prepare(base + 9, g * 6)
                    hidden_low(0, tiles)
                    prepare(base + 10, g * 6)
                    prepare(base + 11, g * 6)
                    hidden(9, g * 6, 1, tiles)
                    hidden_low(1, tiles)
                prepare(base + ffn_chunks)
                accumulate(ffn_chunks, GROUPS - 1)

            ffn_layer("ffn0")
            norm("norm2", chunk0["attn"] + 1)

            dist, neg_log, bias = att["dist"][:], att["neg_log"][:], att["bias"][:]

            def build_tables():
                rest, count = att["scores"][:, 0, :], att["scores"][:, 1, :]
                done = [1]

                def table(ins):
                    ins.then_inc(table_step.sem, 1)
                    done[0] += 1
                    dve.wait_ge(*table_step.at("attn", done[0] - 1))

                dve.wait_ge(*dist_ready.at("attn", 1))
                table(dve.tensor_copy(dist, dist_i[:]))
                for n, (window, dilation) in enumerate(DILATED_GROUPS):
                    this = rest if n else count
                    if dilation == 1:
                        table(dve.tensor_scalar(this, dist, float(window), None, ALU.is_le))
                    else:
                        table(dve.tensor_scalar(bias.bitcast(I32), dist_i[:], dilation - 1, None,
                                                ALU.bitwise_and))
                        table(dve.tensor_scalar(this, bias.bitcast(I32), 0.0, None, ALU.is_equal))
                        if window < SEQ:
                            table(dve.scalar_tensor_tensor(out=this, in0=dist, scalar=float(window),
                                                           in1=this, op0=ALU.is_le, op1=ALU.mult))
                    if n:
                        table(dve.tensor_tensor(count, count, rest, ALU.add))
                table(dve.scalar_tensor_tensor(out=count, in0=dist, scalar=0.0, in1=count,
                                               op0=ALU.is_ge, op1=ALU.mult))
                table(dve.tensor_scalar(neg_log, count, 0.0, MASKED, ALU.is_equal, ALU.mult))
                for c in range(2, len(DILATED_GROUPS) + 1):
                    table(dve.tensor_scalar(rest, count, float(c), -float(np.log(c)),
                                            ALU.is_equal, ALU.mult))
                    table(dve.tensor_tensor(neg_log, neg_log, rest, ALU.add))

            for e in range(2):
                ins = dve.memset(slope[:, e:e + 1], 2.0 ** (-(e + 1) / 2))
            ins.then_inc(slope_ready.sem, 1)

            def project(r, j):
                moving, fixed = r
                part, h = j // 2, j % 2
                cols = slice(h * HALF, (h + 1) * HALF)
                count = moving * 2 + (2 * fixed + h + 1)
                if part == 0:
                    dve.wait_ge(*k_hi_done.at("attn", count))
                    dve.tensor_tensor(att["k_lo"][:, fixed % 2, cols], bank(PROJ + h),
                                      f32(att["k_hi"][:, fixed % 2, cols]), ALU.subtract) \
                       .then_inc(k_lo_done.sem, 1)
                elif part == 2:
                    dve.wait_ge(*q_hi_done.at("attn", count))
                    dve.scalar_tensor_tensor(out=att["q_lo"][:, cols], in0=bank(PROJ + h),
                                             scalar=-float(HD) ** -0.5,
                                             in1=f32(att["q_hi"][:, cols]),
                                             op0=ALU.mult, op1=ALU.subtract) \
                       .then_inc(q_lo_done.sem, 1)

            def values_low(r, h):
                moving, fixed = r
                dve.wait_ge(*vv_hi.at("attn", moving * 2 + (2 * fixed + h + 1)))
                v = att["v_split"][:, fixed % 2, 4 * h:4 * h + 4]
                dve.tensor_tensor(v[:, :, :, HD:P],
                                  bank(VTURN).rearrange("p (j e d) -> p j e d", e=2, d=HD),
                                  f32(v[:, :, :, 0:HD]), ALU.subtract).then_inc(vv_lo.sem, 1)

            def head_bias(moving, fixed, e):
                dve.wait_ge(*slope_ready.at("attn", moving + (fixed + 1)))
                dve.scalar_tensor_tensor(out=bias, in0=dist, scalar=slope[:, e:e + 1],
                                         in1=neg_log, op0=ALU.mult, op1=ALU.add) \
                   .then_inc(bias_ready.sem, 1)
                dve.wait_ge(*bias_ready.at("attn", moving * 2 + (2 * fixed + e + 1)))
                if e:
                    dve.tensor_scalar(slope[:], slope[:], 0.5, None, ALU.mult) \
                       .then_inc(slope_ready.sem, 1)

            def negated_scores(steps, s):
                n = (s % TT + 1) * P
                dve.wait_ge(*s_done.at("attn", steps + (s + 1)))
                dve.wait_ge(*p_turned.at("attn", steps + (s - 1)))
                dve.sem_inc(held, 1)
                dve.tensor_tensor_reduce(
                    out=att["scores"][:, s % 2, 0:n], in0=two_banks(SCORE)[:, 0:n],
                    in1=att["bias"][:, SEQ - n:SEQ], scale=1.0, scalar=3e38,
                    op0=ALU.add, op1=ALU.min,
                    accum_out=neg_max[:, s % 2:s % 2 + 1]).then_inc(max_done.sem, 1)

            def attend(a, after):
                moving, fixed = a
                steps = moving * STEPS + fixed * STEPS
                nxt = (moving, fixed + 1)
                chunk = lambda c: prepare(chunk0["attn"] + 3 * (fixed + 1) + c,
                                          moving if isinstance(moving, int) else moving * 3)

                def probs_low(s):
                    n = (s % TT + 1) * P
                    dve.wait_ge(*ph_done.at("attn", steps + (s + 1)))
                    dve.tensor_tensor(att["pt_lo"][:, s % 2, 0:n], two_banks(PROB)[:, 0:n],
                                      f32(att["pt_hi"][:, s % 2, 0:n]), ALU.subtract) \
                       .then_inc(pl_done.sem, 1)

                def invert(s):
                    dve.wait_ge(*exp_done.at("attn", steps + (s + 1)))
                    dve.wait_ge(*o_done.at("attn", steps + (s - 1)))
                    dve.reciprocal(rden[:, s % 2:s % 2 + 1], den[:, s % 2:s % 2 + 1]) \
                       .then_inc(rden_done.sem, 1)

                for s in range(STEPS):
                    if s + 1 == TT:
                        head_bias(moving, fixed, 1)
                    if s + 1 == STEPS and after:
                        head_bias(moving, fixed + 1, 0)
                    if s + 1 < STEPS or after:
                        negated_scores(steps, s + 1)
                    probs_low(s)
                    invert(s)
                    if not after:
                        continue
                    for c, step in enumerate((1, ends_in[1] + 1, ends_in[3] + 1)):
                        if s == step:
                            chunk(2 + c)
                    for j in range(6):
                        if s == min(ends_in[j] + 1, STEPS - 1):
                            project(nxt, j)
                    for h in range(2):
                        if s == ends_in[2 + h] + 3:
                            values_low(nxt, h)

            prepare(chunk0["attn"] + 2)
            for j in range(6):
                project((0, 0), j)
                if j == 1:
                    build_tables()
                if j in (3, 4):
                    values_low((0, 0), j - 3)
                if j in (1, 3):
                    prepare(chunk0["attn"] + 3 + j // 2)
            head_bias(0, 0, 0)
            negated_scores(0, 0)
            with dve.Fori(0, PAIRS // 2 - 1) as g:
                for pp in range(2):
                    attend((g * 2, pp), True)
            attend((0, PAIRS - 2), True)
            attend((0, PAIRS - 1), False)

            for t in range(TT):
                low_part("oturn", t)
            token_product("oproj")
            norm("norm3")
            ffn_layer("ffn1")
            norm("norm4")

        @block.gpsimd
        def _(pool):
            grant(pool, setup_step, gain_step, dist_ready, mean1_done, rstd1_done, mean2_done, rstd2_done, acc_zero,
                  w_scaled, o_ready)
            step = [0]

            def setup(ins):
                ins.then_inc(setup_step.sem, 1)
                step[0] += 1
                pool.wait_ge(*setup_step.at("norm0", step[0]))

            setup(pool.memset(ones[:], 1.0))
            setup(pool.memset(neg_half[:], -0.5))
            setup(pool.memset(ident[:], 0.0))
            setup(pool.affine_select(out=ident[:], in_=ident[:], compare_op=ALU.not_equal, fill=1.0,
                                     base=0, pattern=[[-1, P]], channel_multiplier=1))

            def inverse_root(sums, means, out_, t, before, mean_sig, rstd_sig, ph):
                pool.wait_ge(*before.at(ph, t + 1))
                pool.tensor_scalar(means[:, t:t + 1], sums[:, t:t + 1], 1.0 / D, EPS,
                                   ALU.mult, ALU.add).then_inc(mean_sig.sem, 1)
                pool.wait_ge(*mean_sig.at(ph, t + 1))
                pool.tensor_tensor(out_[:, t:t + 1], means[:, t:t + 1], neg_half[:], ALU.pow) \
                    .then_inc(rstd_sig.sem, 1)

            def norm(ph):
                post, pre = ph != "norm0", ph != "norm4"
                for i in range(TT + 1):
                    if post and i < TT:
                        inverse_root(square1, mean1, rstd1, i, sq1_done, mean1_done, rstd1_done, ph)
                    t = i - 1 if post else i
                    if pre and 0 <= t < TT:
                        inverse_root(square2, mean2, rstd2, t, sq2_done, mean2_done, rstd2_done, ph)

            def zero_acc(ph, before, before_ph):
                pool.wait_ge(*before.at(before_ph, TT))
                pool.memset(acc[:], 0.0).then_inc(acc_zero.sem, 1)

            norm("norm0")
            norm("norm1")
            pool.wait_ge(*chunk_done.at("conv_out", KT))
            zero_acc("ffn0", x_new, "norm1")
            def scale_chunk(c, moving=0):
                n = chunk0["attn"] + c
                s = n % RAW_RING
                if isinstance(moving, int):
                    pool.wait_ge(raw_in[s], 16 * (n // RAW_RING + 1))
                    gain = gains[:, c, :]
                else:
                    pool.wait_ge(raw_in[s], moving * (16 // RAW_RING) + 16 * (n // RAW_RING + 1))
                    gain = gains[:, bass.ds(moving + c, 1), :].rearrange("p a k -> p (a k)")
                w = by_tile(raw[:, s, :])
                pool.tensor_tensor(w, w, gain.unsqueeze(2).broadcast_to([P, KT, P]), ALU.mult) \
                    .then_inc(w_scaled.sem, 1)

            pool.wait_ge(consts_in, 16 * 5)
            pool.memset(gains[:, 3 * PAIRS:, :], 1.0).then_inc(gain_step.sem, 1)
            by_pair = gains[:, 0:3 * PAIRS, :].rearrange("p (h c) k -> p h c k", c=3)
            for pairs, c, which in ((slice(1, PAIRS), 0, 0), (slice(1, PAIRS), 2, 2),
                                    (slice(0, PAIRS), 1, 0)):
                dst = by_pair[:, pairs, c, :]
                pool.tensor_copy(dst, gains[:, which, :].unsqueeze(1).broadcast_to(dst.shape)) \
                    .then_inc(gain_step.sem, 1)
            pool.wait_ge(*gain_step.at("norm2", 4))
            scale_chunk(0)
            scale_chunk(1)
            norm("norm2")

            pool.wait_ge(*xl_ready.at("norm2", TT))
            pool.iota(dist_i[:], pattern=[[-1, SEQ]], base=SEQ - P, channel_multiplier=1) \
                .then_inc(dist_ready.sem, 1)

            def attend(a, after):
                moving, fixed = a
                for s in range(STEPS):
                    if after:
                        for c, step in enumerate((0, ends_in[1], ends_in[3])):
                            if s == step:
                                scale_chunk(3 * (fixed + 1) + 2 + c,
                                            moving if isinstance(moving, int) else moving * 3)
                    e, i = s // TT, s % TT
                    pool.wait_ge(*o_done.at("attn", moving * STEPS + (fixed * STEPS + s + 1)))
                    if s == 0:
                        pool.wait_ge(spilled, 16)
                    o = att["o_parts"][:, s % 2, :]
                    pool.tensor_tensor(resid[:, i, bass.ds(moving * P + (fixed * P + e * HD), HD)],
                                       o[:, 0:HD], o[:, HD:P], ALU.add).then_inc(o_ready.sem, 1)

            for c in (2, 3, 4):
                scale_chunk(c)
            with pool.Fori(0, PAIRS // 2 - 1) as g:
                for pp in range(2):
                    attend((g * 2, pp), True)
            attend((0, PAIRS - 2), True)
            attend((0, PAIRS - 1), False)
            norm("norm3")
            zero_acc("ffn1", x_new, "norm3")
            norm("norm4")


_INS = ("x", "norm_g", "conv_in_w", "conv_w", "conv_out_w", "kv_norm_g", "kv_w", "q_w", "o_w",
        "ffn_in_w", "ffn_out_w")


def kernel(**inputs):
    import concourse.bacc as bacc
    from concourse.bass_utils import run_bass_kernel_spmd

    nc = bacc.Bacc("TRN2", target_bir_lowering=False, num_devices=1)
    arrays, args = {}, []
    for name in _INS:
        a = np.ascontiguousarray(inputs[name])
        arrays[f"in_{name}"] = a
        args.append(nc.dram_tensor(f"in_{name}", a.shape, mybir.dt.from_np(a.dtype),
                                   kind="ExternalInput").ap())
    shape = tuple(inputs["x"].shape)
    result = nc.dram_tensor("result", shape, F32, kind="ExternalOutput").ap()
    trunk(nc, *args, result)
    r = run_bass_kernel_spmd(nc, [arrays], core_ids=[0])
    return r.results[0]["result"]
```

```python
from contextlib import ExitStack

import numpy as np

import concourse.bass as bass
from concourse import mybir

F32 = mybir.dt.float32
F32R = mybir.dt.float32r
BF16 = mybir.dt.bfloat16
F16 = mybir.dt.float16
I32 = mybir.dt.int32
ALU = mybir.AluOpType
ACT = mybir.ActivationFunctionType

P = 128
HALF = 512
EPS = 1e-6
MASKED = 1e30
DILATED_GROUPS = ((128, 1), (512, 4), (2048, 16))

RAW_RING = 2
SPLIT_RING = 3
CREDIT = 16

PHASES = ("norm0", "conv_in", "conv_out", "norm1", "ffn0", "norm2",
          "attn", "oturn", "oproj", "norm3", "ffn1", "norm4")


class Signal:

    def __init__(self, sem, per_phase):
        self.sem = sem
        self.start = {}
        total = CREDIT
        for ph in PHASES:
            self.start[ph] = total
            total += per_phase.get(ph, 0)

    def at(self, phase, count):
        return self.sem, count + self.start[phase]


def trunk(nc, x, norm_g, conv_in_w, conv_w, conv_out_w, kv_norm_g, kv_w, q_w, o_w,
          ffn_in_w, ffn_out_w, out):
    _, SEQ, D = x.shape
    TT = SEQ // P
    KT = D // P
    DFF = ffn_out_w.shape[1]
    FT = DFF // P
    GROUPS = FT // 2
    HD = 64
    PAIRS = D // P
    STEPS = 2 * TT
    CHUNK = KT * P
    assert SEQ == D == 1024 and FT % 2 == 0 and FT >= 4

    ffn_chunks = 3 * FT
    chunks = {"conv_in": 3 * KT, "conv_out": KT, "ffn0": ffn_chunks, "attn": 3 * PAIRS,
              "oproj": KT, "ffn1": ffn_chunks}
    chunk0 = {}
    total = 0
    for ph in PHASES:
        chunk0[ph] = total
        total += chunks.get(ph, 0)
    CHUNKS = total

    with ExitStack() as ctx:
        sem = lambda name: ctx.enter_context(nc.semaphore(name))

        def place(names):
            made = {}
            with ExitStack() as scope:
                for name, shape, dt in names:
                    made[name] = scope.enter_context(nc.sbuf_tensor(name, [P, *shape], dt))
            return made

        keep = lambda name, shape, dt=F32: ctx.enter_context(nc.sbuf_tensor(name, [P, *shape], dt))

        mix_conv = place([("mix_conv", [KT, SEQ], F32)])["mix_conv"]
        x_lo = keep("x_lo", [KT, SEQ], F32R)
        x_hi = keep("x_hi", [KT, SEQ], F32R)
        resid = keep("resid", [TT, D])
        raw = keep("raw", [RAW_RING, CHUNK])
        w_hi = keep("w_hi", [SPLIT_RING, CHUNK], F32R)
        w_lo = keep("w_lo", [SPLIT_RING, CHUNK], F32R)
        ident = keep("ident", [P])
        neg_half = keep("neg_half", [1])
        taps = keep("taps", [3, KT])
        gains = keep("gains", [3 * PAIRS + 2, KT])
        square0 = keep("square0", [TT])
        square1 = keep("square1", [TT])
        square2 = keep("square2", [TT])
        mean0 = keep("mean0", [TT])
        mean1 = keep("mean1", [TT])
        mean2 = keep("mean2", [TT])
        rstd1 = keep("rstd1", [TT])
        rstd2 = keep("rstd2", [TT])
        slope = keep("slope", [2])
        neg_max = keep("neg_max", [2])
        den = keep("den", [2])
        rden = keep("rden", [2])

        conv = place([("c_gate", [2, HALF], F32), ("u", [SEQ + 2], F32), ("y", [2, HALF], F32),
                      ("y_hi", [KT, SEQ], F32R), ("y_lo", [KT, SEQ], F32R)])
        ffn = place([("g_post", [D], F32),
                     ("junk", [D], BF16),
                     ("xn", [2, D], F32), ("g_pre", [D], F32),
                     ("acc", [TT, D], F32), ("hid_hi", [2, SEQ], F32R), ("hid_lo", [2, SEQ], F32R),
                     ("hid", [2, HALF], F32), ("silu_gate", [2, HALF], F32)])
        dist_i = place([("dist_i", [SEQ], I32)])["dist_i"]
        att = place([("pt", [2, 2, SEQ], F32R),
                     ("q_hi", [SEQ], F32R), ("q_lo", [SEQ], F32R),
                     ("k_hi", [2, SEQ], F32R), ("k_lo", [2, SEQ], F32R),
                     ("v_split", [2, TT, 2, P], F32R),
                     ("dist", [SEQ], F16), ("neg_log", [SEQ], F32), ("bias", [SEQ], F32),
                     ("scores", [2, SEQ], F32), ("v_t", [HALF], F32),
                     ("o_second", [P], F32), ("o_sum", [P], F32),
                     ("o_parts", [2, P], F32)])
        c_gate, u, y, y_hi, y_lo = (conv[n] for n in ("c_gate", "u", "y", "y_hi", "y_lo"))
        junk, xn, g_post, g_pre, acc = (ffn[n] for n in ("junk", "xn", "g_post", "g_pre", "acc"))
        hid_hi, hid_lo, hid, silu_gate = (ffn[n] for n in ("hid_hi", "hid_lo", "hid", "silu_gate"))

        psum = ctx.enter_context(nc.psum_tensor("banks", [P, 8, HALF], F32))
        bank = lambda b: psum[:, b, :]
        two_banks = lambda b: psum[:, b:b + 2, :].rearrange("p a c -> p (a c)")

        x_spill = nc.dram_tensor("x_spill", (TT, P, D), F32, kind="Internal").ap()

        raw_in = [sem(f"raw_in{i}") for i in range(RAW_RING)]
        x_in = [sem(f"x_in{t}") for t in range(TT)]
        consts_in = sem("consts_in")
        post_in, pre_in = sem("post_in"), sem("pre_in")
        held, held_sp = sem("held"), sem("held_sp")
        spilled, x_back, stored = sem("spilled"), sem("x_back"), sem("stored")

        def signal(name, **per_phase):
            return Signal(sem(name), per_phase)

        with_post = {f"norm{i}": TT for i in range(1, 5)}
        with_pre = {f"norm{i}": TT for i in range(4)}
        turned = {**with_pre, "oturn": TT}
        half_done = signal("half_done", conv_in=3 * KT, ffn0=2 * FT, ffn1=2 * FT, attn=3 * PAIRS)
        chunk_done = signal("chunk_done", **chunks)
        tok_done = signal("tok_done", conv_out=2 * (TT - 1), oproj=2 * (TT - 1),
                          ffn0=GROUPS * (2 * TT - 1), ffn1=GROUPS * (2 * TT - 1))
        xt_turned = signal("xt_turned", **turned)
        v_turned = signal("v_turned", attn=2 * PAIRS)
        s_done = signal("s_done", attn=STEPS * PAIRS)
        p_turned = signal("p_turned", attn=STEPS * PAIRS)
        pv_done = signal("pv_done", attn=STEPS * PAIRS)
        o_turned = signal("o_turned", attn=STEPS * PAIRS)
        hi_ready = signal("hi_ready", **chunks)
        c_done = signal("c_done", conv_in=2 * KT)
        yh_done = signal("yh_done", conv_in=2 * KT)
        mix_scaled = signal("mix_scaled", norm1=TT, norm3=TT)
        sq0_done = signal("sq0_done", conv_out=TT, oproj=TT)
        sq1_done = signal("sq1_done", **with_post)
        sq2_done = signal("sq2_done", **with_pre)
        xh_ready = signal("xh_ready", **turned)
        silu_done = signal("silu_done", ffn0=2 * FT, ffn1=2 * FT)
        hh_done = signal("hh_done", ffn0=2 * FT, ffn1=2 * FT)
        k_hi_done = signal("k_hi_done", attn=2 * PAIRS)
        q_hi_done = signal("q_hi_done", attn=2 * PAIRS)
        v_done = signal("v_done", attn=2 * PAIRS)
        vv_hi = signal("vv_hi", attn=2 * PAIRS)
        exp_done = signal("exp_done", attn=STEPS * PAIRS)
        ph_done = signal("ph_done", attn=STEPS * PAIRS)
        second_done = signal("second_done", attn=STEPS * PAIRS)
        o_done = signal("o_done", attn=STEPS * PAIRS)
        lo_ready = signal("lo_ready", **chunks)
        u_done = signal("u_done", conv_in=2 * KT)
        mix_done = signal("mix_done", conv_out=2 * TT, oproj=2 * TT)
        tap_done = signal("tap_done", conv_in=6 * KT)
        ymul_done = signal("ymul_done", conv_in=2 * KT)
        yl_done = signal("yl_done", conv_in=2 * KT)
        x_new_right = signal("x_new_right", norm1=TT, norm3=TT)
        scaled = signal("scaled", norm2=TT, norm4=TT)
        xn_ready = signal("xn_ready", **with_pre)
        xl_ready = signal("xl_ready", **turned)
        hid_done = signal("hid_done", ffn0=2 * FT, ffn1=2 * FT)
        hl_done = signal("hl_done", ffn0=2 * FT, ffn1=2 * FT)
        add_done = signal("add_done", ffn0=GROUPS * 2 * TT, ffn1=GROUPS * 2 * TT)
        table_step = signal("table_step", norm0=1, attn=32)
        bias_ready = signal("bias_ready", attn=2 * PAIRS)
        slope_ready = signal("slope_ready", attn=1 + PAIRS)
        k_lo_done = signal("k_lo_done", attn=2 * PAIRS)
        q_lo_done = signal("q_lo_done", attn=2 * PAIRS)
        vv_lo = signal("vv_lo", attn=2 * PAIRS)
        max_done = signal("max_done", attn=STEPS * PAIRS)
        pl_done = signal("pl_done", attn=STEPS * PAIRS)
        sum_done = signal("sum_done", attn=STEPS * PAIRS)
        rden_done = signal("rden_done", attn=STEPS * PAIRS)
        setup_step = signal("setup_step", norm0=3)
        gain_step = signal("gain_step", norm2=4)
        dist_ready = signal("dist_ready", attn=1)
        mean0_done = signal("mean0_done", conv_out=TT, oproj=TT)
        mean1_done = signal("mean1_done", **with_post)
        x_new = signal("x_new", **with_post)
        rstd1_done = signal("rstd1_done", **with_post)
        mean2_done = signal("mean2_done", **with_pre)
        rstd2_done = signal("rstd2_done", **with_pre)
        acc_zero = signal("acc_zero", ffn0=1, ffn1=1)
        o_ready = signal("o_ready", attn=STEPS * PAIRS)
        w_scaled = signal("w_scaled", attn=chunks["attn"] + 2)

        def grant(eng, *signals):
            for s in signals:
                eng.sem_inc(s.sem, CREDIT)

        tile_of = lambda a, t: a[:, :, t * P:(t + 1) * P]
        by_tile = lambda a: a.rearrange("p (k c) -> p k c", c=P)

        def mixed(ph, t):
            return tile_of(mix_conv, t) if ph == "norm1" else by_tile(acc[:, t, :])

        LEFT = 3
        left = lambda a: a[:, 0:LEFT, :]
        right = lambda a: a[:, LEFT:, :]

        def row(g):
            return g.partition_broadcast(P)

        def turn_bank(ph, t):
            if ph == "oturn":
                return 4 if t == TT - 2 else 6
            if ph == "norm2":
                return 2 * (t % 2)
            return 2 * (t % 2) + 4 * (t // (TT // 2))

        LAG = {"norm0": (0, 0, 0, 2), "norm1": (1, 2, 3, 5), "norm2": (1, 2, 3, 5),
               "norm3": (1, 2, 3, 5), "norm4": (1, 0, 0, 0)}
        AFTER = {"norm1": "conv_out", "norm2": "ffn0", "norm3": "oproj", "norm4": "ffn1"}
        OF_MIXER = ("norm1", "norm3")

        def a_slot(n):
            return n % SPLIT_RING

        block = ctx.enter_context(nc.Block())

        RUN = 3
        PER_HALF = 3 * KT
        RUNS = 6 * PER_HALF // RUN
        slots = [RUNS // STEPS] * STEPS
        END_RUNS = 3
        assert sum(slots) == RUNS
        ends = [sum(slots[:s + 1]) * RUN for s in range(STEPS)]
        ends_in = [next(s for s in range(STEPS) if ends[s] >= (j + 1) * PER_HALF) for j in range(6)]
        SCORE, PROB, OUT, TURN, PROJ = 0, 2, 4, 5, 6

        @block.sync
        def _(sp):
            def column_chunk(w, col):
                return w.rearrange("(k p) n -> p k n", p=P)[:, :, bass.ds(col, P)]

            def load(n, src):
                fixed, moving = n
                s = fixed % RAW_RING
                sp.wait_ge(lo_ready.sem, moving + (fixed - RAW_RING + 1 + CREDIT))
                if not isinstance(moving, int):
                    sp.sem_inc(held_sp, 1)
                sp.dma_start(raw[:, s, :].rearrange("p (k c) -> p k c", c=src.shape[-1])
                             if len(src.shape) == 3 else raw[:, s, :], src).then_inc(raw_in[s], 16)

            def load_two_row_blocks(ph, w):
                for c in range(KT):
                    half, q = c // (KT // 2), c % (KT // 2)
                    load((chunk0[ph] + c, 0),
                         w.rearrange("(k p) n -> p k n", p=P)[:, 2 * q:2 * q + 2,
                                                             half * HALF:(half + 1) * HALF])

            def load_ffn(ph, layer):
                w_in, w_out = ffn_in_w[layer], ffn_out_w[layer]
                base = chunk0[ph]
                for j in range(2):
                    for part in range(2):
                        load((base + 2 * j + part, 0), column_chunk(w_in, part * DFF + j * P))
                with sp.Fori(0, GROUPS - 1) as g:
                    for pos, (what, j) in enumerate((("in", 0), ("in", 0), ("out", 0), ("out", 1),
                                                     ("in", 1), ("in", 1))):
                        n = (base + 4 + pos, g * 6)
                        if what == "in":
                            part = pos % 2
                            load(n, column_chunk(w_in, g * (2 * P) + (2 * P + j * P + part * DFF)))
                        else:
                            load(n, w_out[bass.ds(g * (2 * P) + j * P, P), :])
                for j in range(2):
                    load((base + ffn_chunks - 2 + j, 0),
                         w_out[(FT - 2 + j) * P:(FT - 1 + j) * P, :])

            with nc.allow_non_contiguous_dma("per-feature gains and taps"):
                def load_x(t):
                    sp.dma_start(resid[:, t, :], x[0, t * P:(t + 1) * P, :]).then_inc(x_in[t], 16)

                def load_conv_in(pos, g):
                    f, part = pos // 3, (1, 2, 0)[pos % 3]
                    load((pos, g * 6), column_chunk(conv_in_w[0], g * (2 * P) + (part * D + f * P)))

                load_x(0)
                sp.dma_start(g_pre[:], row(norm_g[0, 0])).then_inc(pre_in, 16)
                for t in range(1, TT // 2):
                    load_x(t)
                load_conv_in(0, 0)
                load_conv_in(1, 0)
                for t in range(TT // 2, TT):
                    load_x(t)
                for j in range(3):
                    sp.dma_start(taps[:, j, :], conv_w[0, j].rearrange("(k p) -> p k", p=P)) \
                        .then_inc(consts_in, 16)
                sp.dma_start(gains[:, 2, :], norm_g[1, 0].rearrange("(k p) -> p k", p=P)) \
                    .then_inc(consts_in, 16)
                sp.dma_start(gains[:, 0, :], kv_norm_g.rearrange("(k p) -> p k", p=P)) \
                    .then_inc(consts_in, 16)

            for pos in range(2, 6):
                load_conv_in(pos, 0)
            with sp.Fori(1, KT // 2) as g:
                for pos in range(6):
                    load_conv_in(pos, g)
            load_two_row_blocks("conv_out", conv_out_w[0])
            load_ffn("ffn0", 0)
            with sp.Fori(0, PAIRS // 2) as g:
                for pos in range(6):
                    col = g * (2 * P) + (pos // 3) * P
                    src = (kv_w, kv_w, q_w[0])[pos % 3]
                    load((chunk0["attn"] + pos, g * 6),
                         column_chunk(src, col + (D if pos % 3 == 1 else 0)))
            load_two_row_blocks("oproj", o_w[0])
            load_ffn("ffn1", 1)
            for t in range(TT):
                sp.wait_ge(*x_new.at("norm4", t + 1))
                sp.dma_start(out[0, t * P:(t + 1) * P, :], resid[:, t, :]).then_inc(stored, 16)
            sp.wait_ge(stored, 16 * TT)

        @block.tensor
        def _(pe):
            grant(pe, half_done, chunk_done, tok_done, xt_turned, v_turned, s_done, p_turned,
                  pv_done, o_turned)

            def weights(n, ph, moving=0):
                pe.wait_ge(*lo_ready.at(ph, moving + n))

            def half_product(slot, out_bank, h, hook=None):
                passes = [(w, a, k) for w, a in ((w_hi, x_hi), (w_hi, x_lo), (w_lo, x_hi))
                          for k in range(KT)]
                for i, (w, a, k) in enumerate(passes):
                    mm = pe.matmul(bank(out_bank), w[:, slot, k * P:(k + 1) * P],
                                   a[:, k, h * HALF:(h + 1) * HALF],
                                   start=(i == 0), stop=(i == len(passes) - 1))
                    if i == len(passes) - 1:
                        mm.then_inc((chunk_done if h else half_done).sem, 1)
                    if hook:
                        hook()

            def feature_product(slot, banks, free):
                for h in range(2):
                    free(h)
                    half_product(slot, banks + h, h)

            def opening(ph, norm_ph):
                weights(2, ph)
                pe.wait_ge(*xl_ready.at(norm_ph, TT // 2))
                count = [0]

                def turn_between():
                    count[0] += 1
                    if count[0] % (3 * KT * 2 // (TT // 2)) == 0:
                        turn(norm_ph, TT // 2 - 1 + count[0] // (3 * KT * 2 // (TT // 2)))

                for c in range(2):
                    half_product(a_slot(chunk0[ph] + c), 2 * c, 0, turn_between)
                pe.wait_ge(*xl_ready.at(norm_ph, TT))
                for c in range(2):
                    half_product(a_slot(chunk0[ph] + c), 2 * c + 1, 1)

            def turn_tile(ph, t, src):
                pe.wait_ge(*xl_ready.at(ph, t if ph == "oturn" and t < TT - 2 else t - 1))
                b = turn_bank(ph, t)
                for k in range(KT):
                    mm = pe.transpose(psum[:, b + k // 4, (k % 4) * P:(k % 4 + 1) * P],
                                      src[:, k * P:(k + 1) * P], ident[:])
                mm.then_inc(xt_turned.sem, 1)

            def turn(ph, t):
                pe.wait_ge(*xn_ready.at(ph, t + 1))
                if ph in OF_MIXER:
                    pe.wait_ge(*mix_done.at(AFTER[ph], TT + turn_bank(ph, t) + 2))
                turn_tile(ph, t, xn[:, t % 2, :])

            def turn_output(t):
                done = TT if t >= TT - 2 else t + 1
                pe.wait_ge(*o_ready.at("attn", STEPS * PAIRS - TT + done))
                turn_tile("oturn", t, resid[:, t, :])

            def token_product(ph, a_hi, a_lo):
                for c in range(KT):
                    half, q = c // (KT // 2), c % (KT // 2)
                    last = q == KT // 2 - 1
                    weights(c + 1, ph)
                    slot = a_slot(chunk0[ph] + c)
                    for t in range(TT):
                        if ph == "oproj" and c == 0:
                            if t in (1, 2):
                                turn_output(TT - 3 + t)
                            pe.wait_ge(*xl_ready.at("oturn", t + 1 if t < TT // 2 else TT))
                        if half and q == 0:
                            pe.wait_ge(*mix_done.at(ph, t + 1))
                        passes = [(a, w, k) for a, w in ((a_hi, w_hi), (a_hi, w_lo), (a_lo, w_hi))
                                  for k in range(2)]
                        for i, (a, w, k) in enumerate(passes):
                            mm = pe.matmul(bank(t), a[:, 2 * q + k, t * P:(t + 1) * P],
                                           w[:, slot, k * HALF:(k + 1) * HALF],
                                           start=(q == 0 and i == 0),
                                           stop=(last and i == len(passes) - 1))
                        if t == TT - 1:
                            mm.then_inc(chunk_done.sem, 1)
                        elif last:
                            mm.then_inc(tok_done.sem, 1)

            pe.wait_ge(*setup_step.at("norm0", 3))
            for t in range(TT // 2):
                turn("norm0", t)

            def conv_in_product(g, pos):
                f = pos // 3
                weights(pos + 1, "conv_in", g * 6)

                def free(h):
                    if pos % 3 == 0:
                        pe.wait_ge(*u_done.at("conv_in", g * 4 + (2 * f - 1 + h)))
                    elif pos % 3 == 1:
                        pe.wait_ge(*ymul_done.at("conv_in", g * 4 + (2 * f - 1 + h)))
                    else:
                        pe.wait_ge(*c_done.at("conv_in", g * 4 + (2 * f + 1 + h)))

                feature_product(a_slot(pos), 2 * (pos % 2), free)

            opening("conv_in", "norm0")
            for pos in range(2, 6):
                conv_in_product(0, pos)
            with pe.Fori(1, KT // 2) as g:
                for pos in range(6):
                    conv_in_product(g, pos)

            pe.wait_ge(*yl_done.at("conv_in", 2 * KT))
            token_product("conv_out", y_hi, y_lo)
            for t in range(TT // 2):
                turn("norm1", t)

            def ffn_layer(ph, norm_ph):
                base = chunk0[ph]

                def in_product(n, moving, j, part, tiles):
                    weights(n - base + 1, ph, moving)

                    def free(h):
                        pe.wait_ge(*(hid_done if part else silu_done).at(ph, tiles + (2 * j - 1 + h)))

                    feature_product(a_slot(n), 2 * part, free)

                def out_product(n, moving, g, turning=False):
                    weights(n - base + 2, ph, moving)
                    pe.wait_ge(*hl_done.at(ph, g * 4 + 4))
                    for o in range(2 * TT):
                        t, h = o // 2, o % 2
                        pe.wait_ge(*add_done.at(ph, g * (2 * TT) + (o - 3)))
                        passes = [(a, w, j) for a, w in ((hid_hi, w_hi), (hid_hi, w_lo),
                                                        (hid_lo, w_hi)) for j in range(2)]
                        for i, (a, w, j) in enumerate(passes):
                            mm = pe.matmul(bank(4 + o % 4), a[:, j, t * P:(t + 1) * P],
                                           w[:, a_slot(n + j), h * HALF:(h + 1) * HALF],
                                           start=(i == 0), stop=(i == len(passes) - 1))
                        if o < 2 * TT - 1:
                            mm.then_inc(tok_done.sem, 1)
                        else:
                            mm.then_inc(chunk_done.sem, 2)
                        if turning and h and t >= TT // 2:
                            turn("norm2", t - TT // 2)

                opening(ph, norm_ph)
                for part in range(2):
                    in_product(base + 2 + part, 0, 1, part, 0)
                with pe.Fori(0, GROUPS - 1) as g:
                    tiles = g * 4 + 4
                    in_product(base + 4, g * 6, 0, 0, tiles)
                    in_product(base + 5, g * 6, 0, 1, tiles)
                    out_product(base + 6, g * 6, g)
                    in_product(base + 8, g * 6, 1, 0, tiles)
                    in_product(base + 9, g * 6, 1, 1, tiles)
                out_product(base + ffn_chunks - 2, 0, GROUPS - 1, turning=(ph == "ffn0"))

            ffn_layer("ffn0", "norm1")

            def project(r, i):
                moving, fixed = r
                j, i = i // PER_HALF, i % PER_HALF
                part, h = j // 2, j % 2
                c = 3 * fixed + part
                if i == 0:
                    if h == 0:
                        pe.wait_ge(*lo_ready.at("attn", moving * 3 + (c + 1)))
                    before = moving * 2 + (2 * fixed + h)
                    if part == 0:
                        pe.wait_ge(*q_lo_done.at("attn", before - 1))
                    elif part == 1:
                        pe.wait_ge(*k_lo_done.at("attn", before + 1))
                    else:
                        pe.wait_ge(*v_done.at("attn", before + 1))
                n, k = i // KT, i % KT
                w, a = ((w_hi, x_hi), (w_hi, x_lo), (w_lo, x_hi))[n]
                mm = pe.matmul(bank(PROJ + h), w[:, a_slot(chunk0["attn"] + c), k * P:(k + 1) * P],
                               a[:, k, h * HALF:(h + 1) * HALF],
                               start=(i == 0), stop=(i == PER_HALF - 1))
                if i == PER_HALF - 1:
                    mm.then_inc((chunk_done if h else half_done).sem, 1)

            def turn_values(r, h):
                moving, fixed = r
                before = moving * 2 + (2 * fixed + h)
                pe.wait_ge(*v_done.at("attn", before + 1))
                pe.wait_ge(*vv_lo.at("attn", before))
                for j in range(4):
                    mm = pe.transpose(psum[:, TURN, j * P:(j + 1) * P],
                                      att["v_t"][:, j * P:(j + 1) * P], ident[:])
                mm.then_inc(v_turned.sem, 1)

            def attend(a, after):
                moving, fixed = a
                parity = fixed % 2
                steps = moving * STEPS + fixed * STEPS
                nxt = (moving, fixed + 1)

                def scores(s):
                    pair, s_in = fixed + s // STEPS, s % STEPS
                    e, i = s_in // TT, s_in % TT
                    rows = slice(HD * e, HD * e + HD)
                    n_keys = (i + 1) * P
                    pe.wait_ge(*max_done.at("attn", steps + s))
                    halves = moving * 2 + (2 * pair + 1 + i // 4)
                    pe.wait_ge(*q_lo_done.at("attn", halves))
                    for lo in range(0, n_keys, HALF):
                        hi = min(lo + HALF, n_keys)
                        passes = (("q_hi", "k_hi"), ("q_hi", "k_lo"), ("q_lo", "k_hi"))
                        for n, (q, k) in enumerate(passes):
                            mm = pe.matmul(psum[:, SCORE + lo // HALF, 0:hi - lo],
                                           att[q][rows, i * P:(i + 1) * P],
                                           att[k][rows, pair % 2, lo:hi],
                                           start=(n == 0), stop=(n == 2))
                    mm.then_inc(s_done.sem, 1)

                def turn_probs(s):
                    i = s % TT
                    pe.wait_ge(*exp_done.at("attn", steps + (s + 1)))
                    pe.wait_ge(*pl_done.at("attn", steps + s))
                    for j in range(i + 1):
                        mm = pe.transpose(psum[:, PROB + j // 4, (j % 4) * P:(j % 4 + 1) * P],
                                          att["scores"][:, s % 2, j * P:(j + 1) * P], ident[:])
                    mm.then_inc(p_turned.sem, 1)

                def outputs(s):
                    e, i = s // TT, s % TT
                    pe.wait_ge(*pl_done.at("attn", steps + (s + 1)))
                    pe.wait_ge(*vv_lo.at("attn", moving * 2 + (2 * fixed + 1 + i // 4)))
                    pe.wait_ge(*sum_done.at("attn", steps + s))
                    for j in range(i + 1):
                        mm = pe.matmul(psum[:, OUT, 0:2 * P].rearrange("p (n q) -> p n q", n=2),
                                       att["v_split"][:, parity, j, e, :],
                                       att["pt"][:, s % 2, :, j * P:(j + 1) * P],
                                       start=(j == 0), stop=(j == i))
                    mm.then_inc(pv_done.sem, 1)

                def turn_part(s):
                    pe.wait_ge(*sum_done.at("attn", steps + (s + 1)))
                    pe.wait_ge(*o_done.at("attn", steps + s))
                    for h in range(2):
                        if after and s == ends_in[2 + h] + 1:
                            pe.wait_ge(*vv_lo.at("attn", moving * 2 + (2 * fixed + 2 + h + 1)))
                    pe.transpose(psum[:, TURN, 0:P], att["o_sum"][:], ident[:]) \
                        .then_inc(o_turned.sem, 1)

                for s in range(STEPS):
                    runs = slots[s] if after else 0
                    first = ends[s] - slots[s] * RUN

                    def fill(r0, r1):
                        for i in range(first + r0 * RUN, first + r1 * RUN):
                            project(nxt, i)

                    if s == STEPS - 1 and after:
                        runs -= END_RUNS
                    third = (runs + 2) // 3
                    if s + 1 < STEPS or after:
                        scores(s + 1)
                    fill(0, min(third, runs))
                    if s >= 2:
                        turn_part(s - 2)
                    turn_probs(s)
                    fill(min(third, runs), min(2 * third, runs))
                    if s >= 1:
                        outputs(s - 1)
                    if after and s in (ends_in[2] + 2, ends_in[3] + 2):
                        pe.wait_ge(*o_done.at("attn", steps + (s - 1)))
                        turn_values(nxt, 0 if s == ends_in[2] + 2 else 1)
                    fill(min(2 * third, runs), runs)
                    if not after and s >= TT + 3:
                        turn_output(s - TT - 3)
                if after:
                    fill(runs, runs + 1)
                turn_part(STEPS - 2)
                if after:
                    fill(runs + 1, runs + 2)
                outputs(STEPS - 1)
                if after:
                    fill(runs + 2, runs + END_RUNS)
                turn_part(STEPS - 1)
                if not after:
                    turn_output(TT - 3)

            pe.wait_ge(*xl_ready.at("norm2", TT // 2))
            for i in range(RUNS * RUN):
                if i and i % (PER_HALF // 4) == 0 and i <= PER_HALF:
                    turn("norm2", TT // 2 - 1 + i // (PER_HALF // 4))
                if i == PER_HALF:
                    pe.wait_ge(*xl_ready.at("norm2", TT))
                if i in (3 * PER_HALF + KT, 4 * PER_HALF + KT):
                    turn_values((0, 0), i // PER_HALF - 3)
                project((0, 0), i)
            pe.wait_ge(*q_lo_done.at("attn", 1))
            for n, (q, k) in enumerate((("q_hi", "k_hi"), ("q_hi", "k_lo"), ("q_lo", "k_hi"))):
                mm = pe.matmul(psum[:, SCORE, 0:P], att[q][0:HD, 0:P], att[k][0:HD, 0, 0:P],
                               start=(n == 0), stop=(n == 2))
            mm.then_inc(s_done.sem, 1)
            with pe.Fori(0, PAIRS // 2 - 1) as g:
                for pp in range(2):
                    attend((g * 2, pp), True)
            attend((0, PAIRS - 2), True)
            attend((0, PAIRS - 1), False)

            token_product("oproj", x_hi, x_lo)
            for t in range(TT // 2):
                turn("norm3", t)
            ffn_layer("ffn1", "norm3")

        @block.scalar
        def _(act):
            grant(act, hi_ready, c_done, yh_done, sq0_done, mix_scaled, sq1_done, sq2_done,
                  xh_ready, silu_done, hh_done, k_hi_done, q_hi_done, v_done, vv_hi, exp_done,
                  ph_done, second_done, o_done)

            def prepare(n, moving=0):
                if n >= CHUNKS:
                    return
                s = n % RAW_RING
                if chunk0["attn"] <= n < chunk0["oproj"] + 2:
                    act.wait_ge(w_scaled.sem, moving + (n - chunk0["attn"] + 1
                                                        + w_scaled.start["attn"]))
                elif isinstance(moving, int):
                    act.wait_ge(raw_in[s], 16 * (n // RAW_RING + 1))
                else:
                    act.wait_ge(raw_in[s], moving * (16 // RAW_RING) + 16 * (n // RAW_RING + 1))
                act.wait_ge(chunk_done.sem, moving + (n - SPLIT_RING + 1 + CREDIT))
                act.copy(w_hi[:, n % SPLIT_RING, :], raw[:, s, :]).then_inc(hi_ready.sem, 1)

            def product(ph, h, a_count, n_count):
                if h == 0:
                    act.wait_ge(*half_done.at(ph, a_count))
                else:
                    act.wait_ge(*chunk_done.at(ph, n_count))

            def high_part(ph, t):
                act.wait_ge(*xt_turned.at(ph, t + 1))
                act.copy(tile_of(x_hi, t), by_tile(two_banks(turn_bank(ph, t)))) \
                    .then_inc(xh_ready.sem, 1)

            last_square = []

            def square(src, sums, done):
                if last_square:
                    act.wait_ge(*last_square[-1])
                junk_out = junk[:, 0:src.shape[-1]] if len(src.shape) == 2 else by_tile(junk[:])
                act.activation(junk_out, src, ACT.Square, accum_out=sums).then_inc(done.sem, 1)

            def norm(ph, late=CHUNKS):
                post, pre = ph != "norm0", ph != "norm4"
                lag1, lag2, _, lag_split = LAG[ph]
                for i in range(TT + lag_split):
                    if ph == "norm0" and i == TT // 2 + 1:
                        prepare(0)
                        prepare(1)
                    if i == TT:
                        prepare(late)
                    if post and i < TT:
                        if ph in OF_MIXER:
                            if i < TT - 1:
                                act.wait_ge(*tok_done.at(AFTER[ph], TT - 1 + i + 1))
                            else:
                                act.wait_ge(*chunk_done.at(AFTER[ph], KT))
                            src = bank(i)
                        else:
                            act.wait_ge(*add_done.at(AFTER[ph], (GROUPS - 1) * 2 * TT + 2 * i + 2))
                            src = acc[:, i, :]
                        square(src, square1[:, i:i + 1], sq1_done)
                        last_square.append(sq1_done.at(ph, i + 1))
                    t = i - lag1
                    if ph in OF_MIXER and 0 <= t < TT:
                        m = left(mixed(ph, t))
                        act.wait_ge(*mix_done.at(AFTER[ph], TT + t + 1))
                        act.wait_ge(*rstd1_done.at(ph, t + 1))
                        act.activation(m, m, ACT.Copy, scale=rstd1[:, t:t + 1]) \
                            .then_inc(mix_scaled.sem, 1)
                    t = i - lag2
                    if pre and 0 <= t < TT:
                        if post:
                            act.wait_ge(*x_new.at(ph, t + 1))
                            if ph in OF_MIXER:
                                act.wait_ge(*x_new_right.at(ph, t + 1))
                        else:
                            act.wait_ge(x_in[t], 16)
                        square(resid[:, t, :], square2[:, t:t + 1], sq2_done)
                        last_square.append(sq2_done.at(ph, t + 1))
                    if pre and i >= lag_split:
                        high_part(ph, i - lag_split)

            def token_product(ph):
                for c in range(KT):
                    prepare(chunk0[ph] + c + 2)
                    if c == KT // 2:
                        act.wait_ge(*chunk_done.at(ph, c + 1))
                        layer = 0 if ph == "conv_out" else 1
                        act.dma_start(g_pre[:], row(norm_g[layer, 2])).then_inc(pre_in, 16)
                    if c != KT // 2 - 1:
                        continue
                    for t in range(TT):
                        if t < TT - 1:
                            act.wait_ge(*tok_done.at(ph, t + 1))
                        else:
                            act.wait_ge(*chunk_done.at(ph, c + 1))
                        square(bank(t), square0[:, t:t + 1], sq0_done)
                        last_square.append(sq0_done.at(ph, t + 1))

            norm("norm0")
            with act.Fori(0, KT // 2) as g:
                for pos in range(6):
                    f = pos // 3
                    prepare(pos + 2, g * 6)
                    for h in range(2):
                        if pos % 3 == 0:
                            product("conv_in", h, g * 6 + (pos + 1), g * 6 + (pos + 1))
                            act.wait_ge(*u_done.at("conv_in", g * 4 + (2 * f - 1 + h)))
                            act.copy(c_gate[:, h, :], bank(2 * (pos % 2) + h)) \
                                .then_inc(c_done.sem, 1)
                        elif pos % 3 == 2:
                            act.wait_ge(*ymul_done.at("conv_in", g * 4 + (2 * f + 1 + h)))
                            act.copy(y_hi[:, g * 2 + f, h * HALF:(h + 1) * HALF], y[:, h, :]) \
                                .then_inc(yh_done.sem, 1)
            act.wait_ge(*u_done.at("conv_in", 2 * KT))
            act.dma_start(g_post[:], row(norm_g[0, 1])).then_inc(post_in, 16)
            token_product("conv_out")
            norm("norm1")

            def ffn_layer(ph):
                base = chunk0[ph]

                def silu(n, moving, j, tiles):
                    for h in range(2):
                        product(ph, h, tiles + (2 * j + 1), moving + (n + 1))
                        act.wait_ge(*hid_done.at(ph, tiles + (2 * j - 1 + h)))
                        act.activation(silu_gate[:, h, :], bank(h), ACT.Silu) \
                            .then_inc(silu_done.sem, 1)

                def hidden_high(j, tiles):
                    for h in range(2):
                        act.wait_ge(*hid_done.at(ph, tiles + (2 * j + 1 + h)))
                        act.copy(hid_hi[:, j, h * HALF:(h + 1) * HALF], hid[:, h, :]) \
                            .then_inc(hh_done.sem, 1)

                act.wait_ge(*x_new.at({"ffn0": "norm1", "ffn1": "norm3"}[ph], TT))
                act.dma_start(g_post[:], row(norm_g[0 if ph == "ffn0" else 1, 3])) \
                    .then_inc(post_in, 16)
                for j in range(2):
                    prepare(base + 2 * j + 2)
                    silu(2 * j, 0, j, 0)
                    prepare(base + 2 * j + 3)
                    hidden_high(j, 0)
                with act.Fori(0, GROUPS - 1) as g:
                    tiles = g * 4 + 4
                    prepare(base + 6, g * 6)
                    silu(4, g * 6, 0, tiles)
                    prepare(base + 7, g * 6)
                    prepare(base + 8, g * 6)
                    act.wait_ge(*chunk_done.at(ph, g * 6 + 8))
                    prepare(base + 9, g * 6)
                    hidden_high(0, tiles)
                    prepare(base + 10, g * 6)
                    silu(8, g * 6, 1, tiles)
                    prepare(base + 11, g * 6)
                    hidden_high(1, tiles)
                prepare(base + ffn_chunks)

            ffn_layer("ffn0")
            norm("norm2", chunk0["attn"] + 1)
            act.dma_start(x_spill.rearrange("t p d -> p t d"), resid[:]).then_inc(spilled, 16)

            def project(r, j):
                moving, fixed = r
                part, h = j // 2, j % 2
                cols = slice(h * HALF, (h + 1) * HALF)
                product("attn", h, moving * 3 + (3 * fixed + part + 1),
                        moving * 3 + (3 * fixed + part + 1))
                if part == 0:
                    act.copy(att["k_hi"][:, fixed % 2, cols], bank(PROJ + h)) \
                        .then_inc(k_hi_done.sem, 1)
                elif part == 1:
                    act.wait_ge(*v_turned.at("attn", moving * 2 + (2 * fixed + h)))
                    act.copy(att["v_t"][:], bank(PROJ + h)).then_inc(v_done.sem, 1)
                else:
                    act.wait_ge(*s_done.at("attn", moving * STEPS
                                           + (fixed * STEPS - (1 - h) * TT // 2)))
                    act.activation(att["q_hi"][:, cols], bank(PROJ + h), ACT.Copy,
                                   scale=-float(HD) ** -0.5).then_inc(q_hi_done.sem, 1)

            def values_high(r, h):
                moving, fixed = r
                act.wait_ge(*v_turned.at("attn", moving * 2 + (2 * fixed + h + 1)))
                act.copy(att["v_split"][:, fixed % 2, 4 * h:4 * h + 4, :, 0:HD],
                         bank(TURN).rearrange("p (j e d) -> p j e d", e=2, d=HD)) \
                    .then_inc(vv_hi.sem, 1)

            def attend(a, after):
                moving, fixed = a
                steps = moving * STEPS + fixed * STEPS
                nxt = (moving, fixed + 1)
                chunk = lambda c: prepare(chunk0["attn"] + 3 * (fixed + 1) + c,
                                          moving if isinstance(moving, int) else moving * 3)

                def probs_high(s):
                    n = (s % TT + 1) * P
                    act.wait_ge(*p_turned.at("attn", steps + (s + 1)))
                    act.wait_ge(*pv_done.at("attn", steps + (s - 1)))
                    act.copy(att["pt"][:, s % 2, 0, 0:n], two_banks(PROB)[:, 0:n]) \
                        .then_inc(ph_done.sem, 1)

                def second_part(s):
                    act.wait_ge(*pv_done.at("attn", steps + (s + 1)))
                    act.wait_ge(*sum_done.at("attn", steps + s))
                    act.copy(att["o_second"][:], psum[:, OUT, P:2 * P]).then_inc(second_done.sem, 1)

                def divide(s):
                    act.wait_ge(*o_turned.at("attn", steps + (s + 1)))
                    act.wait_ge(*rden_done.at("attn", steps + (s + 1)))
                    act.wait_ge(*o_ready.at("attn", steps + (s - 1)))
                    act.activation(att["o_parts"][:, s % 2, :], psum[:, TURN, 0:P],
                                   ACT.Copy, scale=rden[:, s % 2:s % 2 + 1]) \
                        .then_inc(o_done.sem, 1)

                for s in range(STEPS):
                    if not after and s >= TT + 4:
                        high_part("oturn", s - TT - 4)
                    for h in range(2):
                        if after and s == ends_in[2 + h] + 3:
                            values_high(nxt, h)
                    if s >= 2:
                        divide(s - 2)
                    probs_high(s)
                    if s + 1 < STEPS or after:
                        exponentials(steps, s + 1)
                    if s >= 1:
                        second_part(s - 1)
                    if not after:
                        continue
                    for c, step in enumerate((1, ends_in[1] + 1, ends_in[3] + 1)):
                        if s == step:
                            chunk(2 + c)
                    for j in range(6):
                        if s == ends_in[j] + 1:
                            project(nxt, j)
                divide(STEPS - 2)
                second_part(STEPS - 1)
                divide(STEPS - 1)
                if after:
                    project(nxt, 5)
                if not after:
                    for t in range(TT - 4, TT):
                        high_part("oturn", t)

            def exponentials(steps, s):
                n = (s % TT + 1) * P
                act.wait_ge(*max_done.at("attn", steps + (s + 1)))
                act.wait_ge(*rden_done.at("attn", steps + (s - 1)))
                act.activation(att["scores"][:, s % 2, 0:n], att["scores"][:, s % 2, 0:n],
                               ACT.Exp, bias=neg_max[:, s % 2:s % 2 + 1], scale=-1.0,
                               accum_out=den[:, s % 2:s % 2 + 1]).then_inc(exp_done.sem, 1)

            prepare(chunk0["attn"] + 2)
            for j in range(6):
                project((0, 0), j)
                if j in (3, 4):
                    values_high((0, 0), j - 3)
                if j in (1, 3):
                    prepare(chunk0["attn"] + 3 + j // 2)
            exponentials(0, 0)
            with act.Fori(0, PAIRS // 2 - 1) as g:
                for pp in range(2):
                    attend((g * 2, pp), True)
            attend((0, PAIRS - 2), True)
            attend((0, PAIRS - 1), False)

            act.wait_ge(*xl_ready.at("oturn", TT))
            act.wait_ge(spilled, 16)
            act.dma_start(resid[:], x_spill.rearrange("t p d -> p t d")).then_inc(x_back, 16)
            act.dma_start(g_post[:], row(norm_g[1, 1])).then_inc(post_in, 16)
            token_product("oproj")
            norm("norm3")
            ffn_layer("ffn1")
            norm("norm4")

        @block.vector
        def _(dve):
            grant(dve, lo_ready, u_done, tap_done, ymul_done, yl_done, mix_done, x_new_right,
                  scaled, xn_ready,
                  xl_ready, hid_done, hl_done, add_done, table_step, bias_ready, slope_ready,
                  k_lo_done, q_lo_done, vv_lo, max_done, pl_done, sum_done,
                  rden_done)
            f32 = lambda a: a.bitcast(F32)

            def prepare(n, moving=0):
                if n >= CHUNKS:
                    return
                dve.wait_ge(hi_ready.sem, moving + (n + 1 + CREDIT))
                dve.tensor_tensor(w_lo[:, n % SPLIT_RING, :], raw[:, n % RAW_RING, :],
                                  f32(w_hi[:, n % SPLIT_RING, :]), ALU.subtract) \
                   .then_inc(lo_ready.sem, 1)

            def product(ph, h, a_count, n_count):
                if h == 0:
                    dve.wait_ge(*half_done.at(ph, a_count))
                else:
                    dve.wait_ge(*chunk_done.at(ph, n_count))

            def low_part(ph, t):
                dve.wait_ge(*xh_ready.at(ph, t + 1))
                dve.tensor_tensor(tile_of(x_lo, t), by_tile(two_banks(turn_bank(ph, t))),
                                  f32(tile_of(x_hi, t)), ALU.subtract).then_inc(xl_ready.sem, 1)

            posts = {"norm1": 1, "norm2": 2, "norm3": 3, "norm4": 4}
            pres = {"norm0": 1, "norm1": 2, "norm3": 3}

            def take_output(ph, half, t):
                if half:
                    dve.wait_ge(*sq1_done.at({"conv_out": "norm1", "oproj": "norm3"}[ph], t + 1))
                else:
                    dve.wait_ge(*sq0_done.at(ph, t + 1))
                if ph == "conv_out":
                    dst = mix_conv[:, 4 * half:4 * half + 4, t * P:(t + 1) * P]
                else:
                    dst = by_tile(acc[:, t, half * HALF:(half + 1) * HALF])
                dve.tensor_tensor(dst, by_tile(bank(t)),
                                  by_tile(g_post[:, half * HALF:(half + 1) * HALF]),
                                  ALU.mult).then_inc(mix_done.sem, 1)

            def add_output(ph, o, chunks_done, g):
                t, h = o // 2, o % 2
                if o < 2 * TT - 1:
                    dve.wait_ge(*tok_done.at(ph, g * (2 * TT - 1) + (o + 1)))
                else:
                    dve.wait_ge(*chunk_done.at(ph, chunks_done))
                dve.wait_ge(*add_done.at(ph, g * (2 * TT) + (o - 2 * TT + 1)))
                a = acc[:, t, h * HALF:(h + 1) * HALF]
                dve.tensor_tensor(a, a, bank(4 + o % 4), ALU.add).then_inc(add_done.sem, 1)

            def norm(ph, late=CHUNKS):
                post, pre = ph != "norm0", ph != "norm4"
                lag1, _, lag_xn, lag_split = LAG[ph]
                if post:
                    dve.wait_ge(post_in, 16 * posts[ph])
                if ph in pres:
                    dve.wait_ge(pre_in, 16 * pres[ph])
                if ph == "norm3":
                    dve.wait_ge(x_back, 16)
                for i in range(TT + max(lag1, lag_split)):
                    if ph == "norm0" and i == TT // 2 + 1:
                        prepare(0)
                        prepare(1)
                    if i == TT:
                        prepare(late)
                    if ph in OF_MIXER and i < TT:
                        take_output(AFTER[ph], 1, i)
                    elif post and i < TT:
                        for o in (2 * i, 2 * i + 1):
                            add_output(AFTER[ph], o, ffn_chunks, GROUPS - 1)
                    t = i - lag1
                    if ph in OF_MIXER and 0 <= t < TT:
                        dve.wait_ge(*mix_done.at(AFTER[ph], TT + t + 1))
                        dve.wait_ge(*rstd1_done.at(ph, t + 1))
                        x_tile = right(by_tile(resid[:, t, :]))
                        dve.scalar_tensor_tensor(out=x_tile, in0=right(mixed(ph, t)),
                                                 scalar=rstd1[:, t:t + 1], in1=x_tile,
                                                 op0=ALU.mult, op1=ALU.add) \
                           .then_inc(x_new_right.sem, 1)
                    elif post and 0 <= t < TT:
                        m = acc[:, t, :]
                        dve.wait_ge(*rstd1_done.at(ph, t + 1))
                        dve.scalar_tensor_tensor(out=m, in0=m, scalar=rstd1[:, t:t + 1],
                                                 in1=g_post[:], op0=ALU.mult,
                                                 op1=ALU.mult).then_inc(scaled.sem, 1)
                    if pre and i >= lag_split:
                        low_part(ph, i - lag_split)
                    t = i - lag_xn
                    if pre and 0 <= t < TT:
                        dve.wait_ge(*rstd2_done.at(ph, t + 1))
                        dve.wait_ge(*xt_turned.at(ph, t - 1))
                        if ph in pres:
                            ins = dve.scalar_tensor_tensor(out=xn[:, t % 2, :], in0=resid[:, t, :],
                                                           scalar=rstd2[:, t:t + 1], in1=g_pre[:],
                                                           op0=ALU.mult, op1=ALU.mult)
                        else:
                            ins = dve.tensor_scalar(xn[:, t % 2, :], resid[:, t, :],
                                                    rstd2[:, t:t + 1], None, ALU.mult)
                        ins.then_inc(xn_ready.sem, 1)

            def token_product(ph):
                for c in range(KT):
                    prepare(chunk0[ph] + c + 2)
                    if c == KT // 2 - 1:
                        dve.wait_ge(post_in, 16 * (1 if ph == "conv_out" else 3))
                        for t in range(TT):
                            take_output(ph, 0, t)

            norm("norm0")
            dve.wait_ge(*xt_turned.at("norm0", TT))
            dve.memset(u[:, 0:2], 0.0).then_inc(table_step.sem, 1)
            dve.wait_ge(consts_in, 16 * 5)
            dve.wait_ge(*table_step.at("conv_in", 0))
            with dve.Fori(0, KT // 2) as g:
                for pos in range(6):
                    f = pos // 3
                    prepare(pos + 2, g * 6)
                    tap = lambda j: taps[:, j, bass.ds(g * 2 + f, 1)]
                    for h in range(2):
                        count = g * 4 + (2 * f + 1 + h)
                        if pos % 3 == 1:
                            dve.wait_ge(*c_done.at("conv_in", count))
                            product("conv_in", h, g * 6 + (pos + 1), g * 6 + (pos + 1))
                            dve.tensor_tensor(u[:, h * HALF + 2:(h + 1) * HALF + 2],
                                              c_gate[:, h, :], bank(2 * (pos % 2) + h), ALU.mult) \
                               .then_inc(u_done.sem, 1)
                            dve.wait_ge(*u_done.at("conv_in", count))
                            dve.wait_ge(*yh_done.at("conv_in", g * 4 + (2 * f - 1 + h)))
                            for j in range(3):
                                ux = u[:, h * HALF + j:(h + 1) * HALF + j]
                                if j == 0:
                                    ins = dve.tensor_scalar(y[:, h, :], ux, tap(0), None, ALU.mult)
                                else:
                                    dve.wait_ge(*tap_done.at("conv_in", g * 12 + (6 * f + 3 * h + j)))
                                    ins = dve.scalar_tensor_tensor(
                                        out=y[:, h, :], in0=ux, scalar=tap(j), in1=y[:, h, :],
                                        op0=ALU.mult, op1=ALU.add)
                                ins.then_inc(tap_done.sem, 1)
                        elif pos % 3 == 2:
                            product("conv_in", h, g * 6 + (pos + 1), g * 6 + (pos + 1))
                            dve.wait_ge(*tap_done.at("conv_in", g * 12 + (6 * f + 3 * h + 3)))
                            dve.tensor_tensor(y[:, h, :], y[:, h, :], bank(2 * (pos % 2) + h),
                                              ALU.mult).then_inc(ymul_done.sem, 1)
                    if pos % 3 == 2:
                        for h in range(2):
                            cols = slice(h * HALF, (h + 1) * HALF)
                            dve.wait_ge(*yh_done.at("conv_in", g * 4 + (2 * f + 1 + h)))
                            dve.tensor_tensor(y_lo[:, g * 2 + f, cols], y[:, h, :],
                                              f32(y_hi[:, g * 2 + f, cols]), ALU.subtract) \
                               .then_inc(yl_done.sem, 1)
            token_product("conv_out")
            norm("norm1")

            def ffn_layer(ph):
                base = chunk0[ph]

                def hidden(n, moving, j, tiles):
                    for h in range(2):
                        product(ph, h, tiles + (2 * j + 2), moving + (n + 1))
                        dve.wait_ge(*silu_done.at(ph, tiles + (2 * j + 1 + h)))
                        dve.wait_ge(*hl_done.at(ph, tiles + (2 * j - 1 + h)))
                        dve.tensor_tensor(hid[:, h, :], silu_gate[:, h, :], bank(2 + h),
                                          ALU.mult).then_inc(hid_done.sem, 1)

                def hidden_low(j, tiles):
                    for h in range(2):
                        cols = slice(h * HALF, (h + 1) * HALF)
                        dve.wait_ge(*hh_done.at(ph, tiles + (2 * j + 1 + h)))
                        dve.tensor_tensor(hid_lo[:, j, cols], hid[:, h, :],
                                          f32(hid_hi[:, j, cols]), ALU.subtract) \
                           .then_inc(hl_done.sem, 1)

                for j in range(2):
                    prepare(base + 2 * j + 2)
                    prepare(base + 2 * j + 3)
                    hidden(2 * j + 1, 0, j, 0)
                    hidden_low(j, 0)
                dve.wait_ge(*acc_zero.at(ph, 1))
                with dve.Fori(0, GROUPS - 1) as g:
                    tiles = g * 4 + 4
                    prepare(base + 6, g * 6)
                    prepare(base + 7, g * 6)
                    hidden(5, g * 6, 0, tiles)
                    prepare(base + 8, g * 6)
                    for o in range(2 * TT):
                        add_output(ph, o, g * 6 + 8, g)
                    prepare(base + 9, g * 6)
                    hidden_low(0, tiles)
                    prepare(base + 10, g * 6)
                    prepare(base + 11, g * 6)
                    hidden(9, g * 6, 1, tiles)
                    hidden_low(1, tiles)
                prepare(base + ffn_chunks)

            ffn_layer("ffn0")
            norm("norm2", chunk0["attn"] + 1)

            dist, neg_log, bias = att["dist"][:], att["neg_log"][:], att["bias"][:]

            def build_tables():
                rest, count = att["scores"][:, 0, :], att["scores"][:, 1, :]
                done = [1]

                def table(ins):
                    ins.then_inc(table_step.sem, 1)
                    done[0] += 1
                    dve.wait_ge(*table_step.at("attn", done[0] - 1))

                dve.wait_ge(*dist_ready.at("attn", 1))
                table(dve.tensor_copy(dist, dist_i[:]))
                for n, (window, dilation) in enumerate(DILATED_GROUPS):
                    this = rest if n else count
                    if dilation == 1:
                        table(dve.tensor_scalar(this, dist, float(window), None, ALU.is_le))
                    else:
                        table(dve.tensor_scalar(bias.bitcast(I32), dist_i[:], dilation - 1, None,
                                                ALU.bitwise_and))
                        table(dve.tensor_scalar(this, bias.bitcast(I32), 0.0, None, ALU.is_equal))
                        if window < SEQ:
                            table(dve.scalar_tensor_tensor(out=this, in0=dist, scalar=float(window),
                                                           in1=this, op0=ALU.is_le, op1=ALU.mult))
                    if n:
                        table(dve.tensor_tensor(count, count, rest, ALU.add))
                table(dve.scalar_tensor_tensor(out=count, in0=dist, scalar=0.0, in1=count,
                                               op0=ALU.is_ge, op1=ALU.mult))
                table(dve.tensor_scalar(neg_log, count, 0.0, MASKED, ALU.is_equal, ALU.mult))
                for c in range(2, len(DILATED_GROUPS) + 1):
                    table(dve.tensor_scalar(rest, count, float(c), -float(np.log(c)),
                                            ALU.is_equal, ALU.mult))
                    table(dve.tensor_tensor(neg_log, neg_log, rest, ALU.add))

            for e in range(2):
                ins = dve.memset(slope[:, e:e + 1], 2.0 ** (-(e + 1) / 2))
            ins.then_inc(slope_ready.sem, 1)

            def project(r, j):
                moving, fixed = r
                part, h = j // 2, j % 2
                cols = slice(h * HALF, (h + 1) * HALF)
                count = moving * 2 + (2 * fixed + h + 1)
                if part == 0:
                    dve.wait_ge(*k_hi_done.at("attn", count))
                    dve.tensor_tensor(att["k_lo"][:, fixed % 2, cols], bank(PROJ + h),
                                      f32(att["k_hi"][:, fixed % 2, cols]), ALU.subtract) \
                       .then_inc(k_lo_done.sem, 1)
                elif part == 2:
                    dve.wait_ge(*q_hi_done.at("attn", count))
                    dve.scalar_tensor_tensor(out=att["q_lo"][:, cols], in0=bank(PROJ + h),
                                             scalar=-float(HD) ** -0.5,
                                             in1=f32(att["q_hi"][:, cols]),
                                             op0=ALU.mult, op1=ALU.subtract) \
                       .then_inc(q_lo_done.sem, 1)

            def values_low(r, h):
                moving, fixed = r
                dve.wait_ge(*vv_hi.at("attn", moving * 2 + (2 * fixed + h + 1)))
                v = att["v_split"][:, fixed % 2, 4 * h:4 * h + 4]
                dve.tensor_tensor(v[:, :, :, HD:P],
                                  bank(TURN).rearrange("p (j e d) -> p j e d", e=2, d=HD),
                                  f32(v[:, :, :, 0:HD]), ALU.subtract).then_inc(vv_lo.sem, 1)

            def head_bias(moving, fixed, e):
                dve.wait_ge(*slope_ready.at("attn", moving + (fixed + 1)))
                dve.scalar_tensor_tensor(out=bias, in0=dist, scalar=slope[:, e:e + 1],
                                         in1=neg_log, op0=ALU.mult, op1=ALU.add) \
                   .then_inc(bias_ready.sem, 1)
                dve.wait_ge(*bias_ready.at("attn", moving * 2 + (2 * fixed + e + 1)))
                if e:
                    dve.tensor_scalar(slope[:], slope[:], 0.5, None, ALU.mult) \
                       .then_inc(slope_ready.sem, 1)

            def negated_scores(steps, s):
                n = (s % TT + 1) * P
                dve.wait_ge(*s_done.at("attn", steps + (s + 1)))
                dve.wait_ge(*p_turned.at("attn", steps + (s - 1)))
                dve.sem_inc(held, 1)
                dve.tensor_tensor_reduce(
                    out=att["scores"][:, s % 2, 0:n], in0=two_banks(SCORE)[:, 0:n],
                    in1=att["bias"][:, SEQ - n:SEQ], scale=1.0, scalar=3e38,
                    op0=ALU.add, op1=ALU.min,
                    accum_out=neg_max[:, s % 2:s % 2 + 1]).then_inc(max_done.sem, 1)

            def attend(a, after):
                moving, fixed = a
                steps = moving * STEPS + fixed * STEPS
                nxt = (moving, fixed + 1)
                chunk = lambda c: prepare(chunk0["attn"] + 3 * (fixed + 1) + c,
                                          moving if isinstance(moving, int) else moving * 3)

                def probs_low(s):
                    n = (s % TT + 1) * P
                    dve.wait_ge(*ph_done.at("attn", steps + (s + 1)))
                    dve.tensor_tensor(att["pt"][:, s % 2, 1, 0:n], two_banks(PROB)[:, 0:n],
                                      f32(att["pt"][:, s % 2, 0, 0:n]), ALU.subtract) \
                       .then_inc(pl_done.sem, 1)

                def invert(s):
                    dve.wait_ge(*exp_done.at("attn", steps + (s + 1)))
                    dve.wait_ge(*o_done.at("attn", steps + (s - 1)))
                    dve.reciprocal(rden[:, s % 2:s % 2 + 1], den[:, s % 2:s % 2 + 1]) \
                       .then_inc(rden_done.sem, 1)

                def sum_parts(s):
                    dve.wait_ge(*second_done.at("attn", steps + (s + 1)))
                    dve.wait_ge(*o_turned.at("attn", steps + s))
                    dve.tensor_tensor(att["o_sum"][:], psum[:, OUT, 0:P], att["o_second"][:],
                                      ALU.add).then_inc(sum_done.sem, 1)

                for s in range(STEPS):
                    for h in range(2):
                        if after and s == ends_in[2 + h] + 3:
                            values_low(nxt, h)
                    if s + 1 == TT or s + 1 == STEPS and after:
                        dve.wait_ge(*max_done.at("attn", steps + (s + 1)))
                        head_bias(moving, fixed + (s + 1) // STEPS, (s + 1) // TT % 2)
                    if s + 1 < STEPS or after:
                        negated_scores(steps, s + 1)
                    if not after and s >= TT + 4:
                        low_part("oturn", s - TT - 4)
                    probs_low(s)
                    invert(s)
                    if s >= 1:
                        sum_parts(s - 1)
                    if not after:
                        continue
                    for c, step in enumerate((1, ends_in[1] + 1, ends_in[3] + 1)):
                        if s == step:
                            chunk(2 + c)
                    for j in range(6):
                        if s == ends_in[j] + 1:
                            project(nxt, j)
                sum_parts(STEPS - 1)
                if after:
                    project(nxt, 5)

            prepare(chunk0["attn"] + 2)
            for j in range(6):
                project((0, 0), j)
                if j == 1:
                    build_tables()
                if j in (3, 4):
                    values_low((0, 0), j - 3)
                if j in (1, 3):
                    prepare(chunk0["attn"] + 3 + j // 2)
            head_bias(0, 0, 0)
            negated_scores(0, 0)
            with dve.Fori(0, PAIRS // 2 - 1) as g:
                for pp in range(2):
                    attend((g * 2, pp), True)
            attend((0, PAIRS - 2), True)
            attend((0, PAIRS - 1), False)
            for t in range(TT - 4, TT):
                low_part("oturn", t)
            token_product("oproj")
            norm("norm3")
            ffn_layer("ffn1")
            norm("norm4")

        @block.gpsimd
        def _(pool):
            grant(pool, setup_step, gain_step, dist_ready, mean0_done, mean1_done, rstd1_done,
                  x_new, mean2_done, rstd2_done, acc_zero, w_scaled, o_ready)
            step = [0]

            def setup(ins):
                ins.then_inc(setup_step.sem, 1)
                step[0] += 1
                pool.wait_ge(*setup_step.at("norm0", step[0]))

            setup(pool.memset(neg_half[:], -0.5))
            setup(pool.memset(ident[:], 0.0))
            setup(pool.affine_select(out=ident[:], in_=ident[:], compare_op=ALU.not_equal, fill=1.0,
                                     base=0, pattern=[[-1, P]], channel_multiplier=1))

            def inverse_root(sums, means, out_, t, before, mean_sig, rstd_sig, ph):
                pool.wait_ge(*before.at(ph, t + 1))
                pool.tensor_scalar(means[:, t:t + 1], sums[:, t:t + 1], 1.0 / D, EPS,
                                   ALU.mult, ALU.add).then_inc(mean_sig.sem, 1)
                root(means, out_, t, mean_sig, rstd_sig, ph)

            def root(means, out_, t, mean_sig, rstd_sig, ph):
                pool.wait_ge(*mean_sig.at(ph, t + 1))
                pool.tensor_tensor(out_[:, t:t + 1], means[:, t:t + 1], neg_half[:], ALU.pow) \
                    .then_inc(rstd_sig.sem, 1)

            def first_means(ph):
                for t in range(TT):
                    pool.wait_ge(*sq0_done.at(ph, t + 1))
                    pool.tensor_scalar(mean0[:, t:t + 1], square0[:, t:t + 1], 1.0 / D, EPS,
                                       ALU.mult, ALU.add).then_inc(mean0_done.sem, 1)

            def norm(ph):
                post, pre = ph != "norm0", ph != "norm4"
                lag1, lag2, _, _ = LAG[ph]
                if ph == "norm3":
                    pool.wait_ge(x_back, 16)
                for i in range(TT + max(lag1, lag2)):
                    if post and i < TT:
                        if ph in OF_MIXER:
                            pool.wait_ge(*sq1_done.at(ph, i + 1))
                            pool.wait_ge(*mean0_done.at(AFTER[ph], i + 1))
                            pool.tensor_scalar(mean1[:, i:i + 1], square1[:, i:i + 1], 1.0 / D,
                                               mean0[:, i:i + 1], ALU.mult, ALU.add) \
                                .then_inc(mean1_done.sem, 1)
                            root(mean1, rstd1, i, mean1_done, rstd1_done, ph)
                        else:
                            inverse_root(square1, mean1, rstd1, i, sq1_done, mean1_done,
                                         rstd1_done, ph)
                    t = i - lag1
                    if post and 0 <= t < TT:
                        pool.wait_ge(*(mix_scaled if ph in OF_MIXER else scaled).at(ph, t + 1))
                        part = left if ph in OF_MIXER else lambda a: a
                        m = part(mixed(ph, t))
                        x_tile = part(by_tile(resid[:, t, :]))
                        pool.tensor_tensor(x_tile, x_tile, m, ALU.add).then_inc(x_new.sem, 1)
                    t = i - lag2
                    if pre and 0 <= t < TT:
                        inverse_root(square2, mean2, rstd2, t, sq2_done, mean2_done, rstd2_done, ph)

            def zero_acc(ph, before, before_ph):
                pool.wait_ge(*before.at(before_ph, TT))
                pool.memset(acc[:], 0.0).then_inc(acc_zero.sem, 1)

            norm("norm0")
            first_means("conv_out")
            norm("norm1")
            pool.wait_ge(*chunk_done.at("conv_out", KT))
            zero_acc("ffn0", x_new, "norm1")

            def scale_chunk(c, moving=0):
                n = chunk0["attn"] + c
                s = n % RAW_RING
                if isinstance(moving, int):
                    pool.wait_ge(raw_in[s], 16 * (n // RAW_RING + 1))
                    gain = gains[:, c, :]
                else:
                    pool.wait_ge(raw_in[s], moving * (16 // RAW_RING) + 16 * (n // RAW_RING + 1))
                    gain = gains[:, bass.ds(moving + c, 1), :].rearrange("p a k -> p (a k)")
                w = by_tile(raw[:, s, :])
                pool.tensor_tensor(w, w, gain.unsqueeze(2).broadcast_to([P, KT, P]), ALU.mult) \
                    .then_inc(w_scaled.sem, 1)

            pool.wait_ge(consts_in, 16 * 5)
            pool.memset(gains[:, 3 * PAIRS:, :], 1.0).then_inc(gain_step.sem, 1)
            by_pair = gains[:, 0:3 * PAIRS, :].rearrange("p (h c) k -> p h c k", c=3)
            for pairs, c, which in ((slice(1, PAIRS), 0, 0), (slice(1, PAIRS), 2, 2),
                                    (slice(0, PAIRS), 1, 0)):
                dst = by_pair[:, pairs, c, :]
                pool.tensor_copy(dst, gains[:, which, :].unsqueeze(1).broadcast_to(dst.shape)) \
                    .then_inc(gain_step.sem, 1)
            pool.wait_ge(*gain_step.at("norm2", 4))
            scale_chunk(0)
            scale_chunk(1)
            norm("norm2")

            pool.wait_ge(*xl_ready.at("norm2", TT))
            pool.iota(dist_i[:], pattern=[[-1, SEQ]], base=SEQ - P, channel_multiplier=1) \
                .then_inc(dist_ready.sem, 1)

            def attend(a, after):
                moving, fixed = a
                for s in range(STEPS):
                    if after:
                        for c, step in enumerate((0, ends_in[1], ends_in[3])):
                            if s == step:
                                scale_chunk(3 * (fixed + 1) + 2 + c,
                                            moving if isinstance(moving, int) else moving * 3)
                    e, i = s // TT, s % TT
                    pool.wait_ge(*o_done.at("attn", moving * STEPS + (fixed * STEPS + s + 1)))
                    if s == 0:
                        pool.wait_ge(spilled, 16)
                    o = att["o_parts"][:, s % 2, :]
                    pool.tensor_tensor(resid[:, i, bass.ds(moving * P + (fixed * P + e * HD), HD)],
                                       o[:, 0:HD], o[:, HD:P], ALU.add).then_inc(o_ready.sem, 1)

            for c in (2, 3, 4):
                scale_chunk(c)
            with pool.Fori(0, PAIRS // 2 - 1) as g:
                for pp in range(2):
                    attend((g * 2, pp), True)
            attend((0, PAIRS - 2), True)
            attend((0, PAIRS - 1), False)
            first_means("oproj")
            norm("norm3")
            zero_acc("ffn1", x_new, "norm3")
            norm("norm4")


_INS = ("x", "norm_g", "conv_in_w", "conv_w", "conv_out_w", "kv_norm_g", "kv_w", "q_w", "o_w",
        "ffn_in_w", "ffn_out_w")


def kernel(**inputs):
    import concourse.bacc as bacc
    from concourse.bass_utils import run_bass_kernel_spmd

    nc = bacc.Bacc("TRN2", target_bir_lowering=False, num_devices=1)
    arrays, args = {}, []
    for name in _INS:
        a = np.ascontiguousarray(inputs[name])
        arrays[f"in_{name}"] = a
        args.append(nc.dram_tensor(f"in_{name}", a.shape, mybir.dt.from_np(a.dtype),
                                   kind="ExternalInput").ap())
    shape = tuple(inputs["x"].shape)
    result = nc.dram_tensor("result", shape, F32, kind="ExternalOutput").ap()
    trunk(nc, *args, result)
    r = run_bass_kernel_spmd(nc, [arrays], core_ids=[0])
    return r.results[0]["result"]
```
